# Optimizing a Trainium2 kernel written in Bass

```python
import math
import jax, jax.numpy as jnp
from jax import lax
import numpy as np

D_MODEL = 1024
BATCH = 1
SEQ = 128
DEPTH = 2
DEC_BATCH = 1
DEC_SEQ = 512
PAST_LEN = 128

GRID_W = 64
N_MIXERS = 4
N_DELTA = len(range(0, DEPTH, N_MIXERS))
N_CONV = len(range(1, DEPTH, N_MIXERS))
N_FOURIER = len(range(2, DEPTH, N_MIXERS))
N_POOL = len(range(3, DEPTH, N_MIXERS))
N_DENSE = len(range(0, DEPTH, 2))
N_MOE = len(range(1, DEPTH, 2))

LIN_HEADS = 8
LIN_DK = 128
LIN_DV = 128
LIN_QK = LIN_HEADS * LIN_DK
LIN_V = LIN_HEADS * LIN_DV
CHUNK = 64
SHORT_CONV = 3
FOURIER_GROUPS = 4
POOL_WINDOWS = (2, 4, 8, 16)
POOL_GROUP = D_MODEL // len(POOL_WINDOWS)
D_FF = 2816
N_EXPERTS = 8
TOP_K = 2
D_EXPERT = 1408
NORM_EPS = 1e-6

kernel_name = "hybrid_deltanet_conv_fourier_pool_dit_step"

def rmsnorm(x, w):
    xf = x.astype(jnp.float32)
    y = xf * lax.rsqrt(jnp.mean(xf * xf, axis=-1, keepdims=True) + NORM_EPS)
    return (y * w.astype(jnp.float32)).astype(x.dtype)

def l2norm(x):
    xf = x.astype(jnp.float32)
    return (xf * lax.rsqrt(jnp.sum(xf * xf, axis=-1, keepdims=True) + NORM_EPS)).astype(x.dtype)

def local_op(fn, x, grid, *args):
    if not grid:
        return fn(x, *args)
    b, n, ch = x.shape
    rows = n // GRID_W
    return fn(x.reshape(b * rows, GRID_W, ch), *args).reshape(b, n, ch)

def dwconv_centred(x, w):
    k = w.shape[0]
    r = k // 2
    n = x.shape[-2]
    xp = jnp.pad(x, [(0, 0)] * (x.ndim - 2) + [(r, r), (0, 0)])
    y = xp[..., 0:n, :] * w[0]
    for j in range(1, k):
        y = y + xp[..., j:j + n, :] * w[j]
    return y

def pool_minus(x, win):
    n = x.shape[-2]
    t = np.arange(n)
    lo = np.clip(t - win // 2, 0, n - 1)
    hi = np.clip(t + win // 2 - 1, 0, n - 1)
    xf = x.astype(jnp.float32)
    csum = jnp.pad(jnp.cumsum(xf, axis=-2), [(0, 0)] * (x.ndim - 2) + [(1, 0), (0, 0)])
    s = jnp.take(csum, hi + 1, axis=-2) - jnp.take(csum, lo, axis=-2)
    cnt = jnp.asarray(hi - lo + 1, jnp.float32)[:, None]
    return (s / cnt - xf).astype(x.dtype)

def chunk_gated_delta(q, k, v, g, beta, s0):
    out_dtype = v.dtype
    f32 = jnp.float32
    b, n_tok, h, dk = q.shape
    dv = v.shape[-1]
    n = n_tok // CHUNK

    def blocks(t):
        return jnp.moveaxis(t.astype(f32).reshape(b, n, CHUNK, h, -1), 3, 1)

    def blocks_h(t):
        return jnp.moveaxis(t.astype(f32).reshape(b, n, CHUNK, h), 3, 1)

    qc = blocks(q) * (dk ** -0.5)
    kc = blocks(k)
    vc = blocks(v)
    bc = blocks_h(beta)
    gc = jnp.cumsum(blocks_h(g), axis=-1)
    incl = np.tril(np.ones((CHUNK, CHUNK), bool))
    strict = np.tril(np.ones((CHUNK, CHUNK), bool), -1)
    diff = gc[..., :, None] - gc[..., None, :]
    decay = jnp.where(incl, jnp.exp(jnp.where(incl, diff, 0.0)), 0.0)
    kb = kc * bc[..., None]
    lmat = jnp.where(strict, jnp.einsum('bhncd,bhnsd->bhncs', kb, kc) * decay, 0.0)
    rhs = jnp.concatenate([vc * bc[..., None], kb * jnp.exp(gc)[..., None]], axis=-1)
    sol = lax.linalg.triangular_solve(lmat + jnp.eye(CHUNK, dtype=f32), rhs, left_side=True, lower=True)
    u, w = sol[..., :dv], sol[..., dv:]
    intra = jnp.where(incl, jnp.einsum('bhncd,bhnsd->bhncs', qc, kc) * decay, 0.0)
    xs = tuple(jnp.moveaxis(t, 2, 0) for t in (qc, kc, u, w, gc, intra))

    def step(state, inp):
        q_i, k_i, u_i, w_i, g_i, a_i = inp
        v_new = u_i - jnp.einsum('bhcd,bhde->bhce', w_i, state)
        o_i = (jnp.einsum('bhcd,bhde->bhce', q_i * jnp.exp(g_i)[..., None], state)
               + jnp.einsum('bhcs,bhse->bhce', a_i, v_new))
        g_last = g_i[..., -1:]
        state = (state * jnp.exp(g_last)[..., None]
                 + jnp.einsum('bhcd,bhce->bhde', k_i * jnp.exp(g_last - g_i)[..., None], v_new))
        return state, o_i

    s_fin, o = lax.scan(step, s0.astype(f32), xs)
    o = jnp.transpose(o, (1, 0, 3, 2, 4)).reshape(b, n_tok, h, dv)
    return o.astype(out_dtype), s_fin.astype(out_dtype)

def deltanet_mixer(x, w_in, conv_w, a_log, dt_bias, norm_w, w_out, s0_f, s0_b, grid):
    b, n, _ = x.shape
    proj = x @ w_in
    qkv = jax.nn.silu(local_op(dwconv_centred, proj[..., :2 * LIN_QK + LIN_V], grid, conv_w))
    q = l2norm(qkv[..., :LIN_QK].reshape(b, n, LIN_HEADS, LIN_DK))
    k = l2norm(qkv[..., LIN_QK:2 * LIN_QK].reshape(b, n, LIN_HEADS, LIN_DK))
    v = qkv[..., 2 * LIN_QK:].reshape(b, n, LIN_HEADS, LIN_DV)
    z = proj[..., 2 * LIN_QK + LIN_V:2 * LIN_QK + 2 * LIN_V].reshape(b, n, LIN_HEADS, LIN_DV)
    ab = proj[..., 2 * LIN_QK + 2 * LIN_V:].astype(jnp.float32).reshape(b, n, 4, LIN_HEADS)
    g = -jnp.exp(a_log.astype(jnp.float32)) * jax.nn.softplus(ab[:, :, 0:2] + dt_bias.astype(jnp.float32))
    beta = jax.nn.sigmoid(ab[:, :, 2:4])
    o_f, s_f = chunk_gated_delta(q, k, v, g[:, :, 0], beta[:, :, 0], s0_f)
    rev = lambda t: jnp.flip(t, axis=1)
    o_b, s_b = chunk_gated_delta(rev(q), rev(k), rev(v), rev(g[:, :, 1]), rev(beta[:, :, 1]), s0_b)
    o = o_f + rev(o_b)
    o = rmsnorm(o, norm_w) * jax.nn.silu(z)
    return o.reshape(b, n, LIN_V) @ w_out, s_f, s_b

def shortconv_mixer(x, w_in, conv_w, w_out, grid):
    gate_b, gate_c, u = jnp.split(x @ w_in, 3, axis=-1)
    y = gate_b * local_op(dwconv_centred, gate_c * u, grid, conv_w)
    return y @ w_out

def fourier_mixer(x, w_out):
    b, n, d = x.shape
    xg = x.astype(jnp.float32).reshape(b, n, FOURIER_GROUPS, d // FOURIER_GROUPS)
    f = jnp.fft.fft2(xg, axes=(1, 3), norm="ortho").real
    return f.astype(x.dtype).reshape(b, n, d) @ w_out

def pooling_mixer(x, group_w, scale, grid):
    outs = []
    for gi, win in enumerate(POOL_WINDOWS):
        xg = x[..., gi * POOL_GROUP:(gi + 1) * POOL_GROUP]
        outs.append(local_op(pool_minus, xg, grid, win) @ group_w[gi])
    return jnp.concatenate(outs, axis=-1) * scale

def swiglu(x, w13, w2):
    gate, up = jnp.split(x @ w13, 2, axis=-1)
    return (jax.nn.silu(gate) * up) @ w2

def moe_swiglu(x, router_w, router_b, w13, w2):
    b, n, d = x.shape
    t = x.reshape(b * n, d)
    logits = (t @ router_w).astype(jnp.float32) + router_b.astype(jnp.float32)
    probs = jax.nn.softmax(logits, axis=-1)
    top_p, top_i = lax.top_k(probs, TOP_K)
    top_p = top_p / jnp.sum(top_p, axis=-1, keepdims=True)
    gates = jnp.einsum('tk,tke->te', top_p, jax.nn.one_hot(top_i, N_EXPERTS, dtype=jnp.float32)).astype(x.dtype)
    out = jnp.zeros_like(t)
    for e in range(N_EXPERTS):
        out = out + gates[:, e:e + 1] * swiglu(t, w13[e], w2[e])
    return out.reshape(b, n, d)

def trunk(x, cond, init_f, init_b, grid, p):
    nb = x.shape[0]
    fin_f, fin_b = [], []
    for i in range(DEPTH):
        mod = jax.nn.silu(cond) @ p["mod_w"][i] + p["mod_b"][i]
        sh1, sc1, g1, sh2, sc2, g2 = jnp.split(mod[:, None, :], 6, axis=-1)
        h = rmsnorm(x, p["norm_w"][i, 0]) * (1 + sc1) + sh1
        kind, j = i % N_MIXERS, i // N_MIXERS
        if kind == 0:
            if init_f is None:
                zero = jnp.zeros((nb, LIN_HEADS, LIN_DK, LIN_DV), x.dtype)
                s0f, s0b = zero, zero
            else:
                s0f, s0b = init_f[:, j], init_b[:, j]
            y, sf, sb = deltanet_mixer(h, p["dn_w_in"][j], p["dn_conv"][j], p["dn_a_log"][j],
                                       p["dn_dt_bias"][j], p["dn_norm"][j], p["dn_w_out"][j],
                                       s0f, s0b, grid)
            fin_f.append(sf)
            fin_b.append(sb)
        elif kind == 1:
            y = shortconv_mixer(h, p["sc_w_in"][j], p["sc_conv"][j], p["sc_w_out"][j], grid)
        elif kind == 2:
            y = fourier_mixer(h, p["fn_w_out"][j])
        else:
            y = pooling_mixer(h, p["pl_w"][j], p["pl_scale"][j], grid)
        x = x + g1 * y
        h = rmsnorm(x, p["norm_w"][i, 1]) * (1 + sc2) + sh2
        if i % 2 == 0:
            y = swiglu(h, p["ffn_w13"][i // 2], p["ffn_w2"][i // 2])
        else:
            y = moe_swiglu(h, p["moe_router"][i // 2], p["moe_router_b"][i // 2],
                           p["moe_w13"][i // 2], p["moe_w2"][i // 2])
        x = x + g2 * y
    return rmsnorm(x, p["final_norm"]), jnp.stack(fin_f, axis=1), jnp.stack(fin_b, axis=1)

def setup_inputs(seed: int = 0) -> dict:
    key = jax.random.key(seed)
    ks = iter(jax.random.split(key, 40))
    f32 = jnp.float32
    D = D_MODEL
    H = LIN_HEADS

    def nrm(shape, scale):
        return jax.random.normal(next(ks), shape, f32) * scale

    dt = jnp.exp(jax.random.uniform(next(ks), (N_DELTA, 2, H), f32, math.log(1e-3), math.log(0.1)))
    dt_bias = dt + jnp.log(-jnp.expm1(-dt))
    a_log = jnp.log(jax.random.uniform(next(ks), (N_DELTA, 2, H), f32, 1.0, 16.0))
    return {
        "x_prompt": nrm((BATCH, SEQ, D), 1.0),
        "x_sample": nrm((DEC_BATCH, DEC_SEQ, D), 1.0),
        "state_fwd": nrm((DEC_BATCH, N_DELTA, H, LIN_DK, LIN_DV), 0.2),
        "state_bwd": nrm((DEC_BATCH, N_DELTA, H, LIN_DK, LIN_DV), 0.2),
        "c": nrm((DEC_BATCH, D), 1.0),
        "c_ctx": nrm((D,), 1.0),
        "norm_w": 1.0 + nrm((DEPTH, 2, D), 0.05),
        "mod_w": nrm((DEPTH, D, 6 * D), 0.5 * D ** -0.5),
        "mod_b": nrm((DEPTH, 6 * D), 0.02),
        "dn_w_in": nrm((N_DELTA, D, 2 * LIN_QK + 2 * LIN_V + 4 * H), D ** -0.5),
        "dn_conv": nrm((N_DELTA, SHORT_CONV, 2 * LIN_QK + LIN_V), SHORT_CONV ** -0.5),
        "dn_a_log": a_log,
        "dn_dt_bias": dt_bias,
        "dn_norm": 1.0 + nrm((N_DELTA, LIN_DV), 0.05),
        "dn_w_out": nrm((N_DELTA, LIN_V, D), LIN_V ** -0.5),
        "sc_w_in": nrm((N_CONV, D, 3 * D), D ** -0.5),
        "sc_conv": nrm((N_CONV, SHORT_CONV, D), SHORT_CONV ** -0.5),
        "sc_w_out": nrm((N_CONV, D, D), D ** -0.5),
        "fn_w_out": nrm((N_FOURIER, D, D), D ** -0.5),
        "pl_w": nrm((N_POOL, len(POOL_WINDOWS), POOL_GROUP, POOL_GROUP), POOL_GROUP ** -0.5),
        "pl_scale": 1.0 + nrm((N_POOL, D), 0.1),
        "ffn_w13": nrm((N_DENSE, D, 2 * D_FF), D ** -0.5),
        "ffn_w2": nrm((N_DENSE, D_FF, D), D_FF ** -0.5),
        "moe_router": nrm((N_MOE, D, N_EXPERTS), D ** -0.5),
        "moe_router_b": nrm((N_MOE, N_EXPERTS), 0.01),
        "moe_w13": nrm((N_MOE, N_EXPERTS, D, 2 * D_EXPERT), D ** -0.5),
        "moe_w2": nrm((N_MOE, N_EXPERTS, D_EXPERT, D), D_EXPERT ** -0.5),
        "final_norm": 1.0 + nrm((D,), 0.05),
    }

def reference(x_prompt, x_sample, state_fwd, state_bwd, c, c_ctx, norm_w, mod_w, mod_b,
              dn_w_in, dn_conv, dn_a_log, dn_dt_bias, dn_norm, dn_w_out,
              sc_w_in, sc_conv, sc_w_out, fn_w_out, pl_w, pl_scale,
              ffn_w13, ffn_w2, moe_router, moe_router_b, moe_w13, moe_w2, final_norm):
    params = dict(norm_w=norm_w, mod_w=mod_w, mod_b=mod_b,
                  dn_w_in=dn_w_in, dn_conv=dn_conv, dn_a_log=dn_a_log, dn_dt_bias=dn_dt_bias,
                  dn_norm=dn_norm, dn_w_out=dn_w_out,
                  sc_w_in=sc_w_in, sc_conv=sc_conv, sc_w_out=sc_w_out,
                  fn_w_out=fn_w_out, pl_w=pl_w, pl_scale=pl_scale,
                  ffn_w13=ffn_w13, ffn_w2=ffn_w2,
                  moe_router=moe_router, moe_router_b=moe_router_b, moe_w13=moe_w13, moe_w2=moe_w2,
                  final_norm=final_norm)
    y_prompt, new_state_fwd, new_state_bwd = trunk(x_prompt, c_ctx[None, :], None, None, False, params)
    y_sample, _, _ = trunk(x_sample, c, state_fwd, state_bwd, True, params)
    return (y_prompt, y_sample, new_state_fwd, new_state_bwd)


_drawn_inputs = setup_inputs


def setup_inputs(seed=0):
    import zlib

    import numpy as np

    out = dict(_drawn_inputs(seed))
    spreads = {}
    factors = {'dn_norm': 3.878, 'moe_router_b': 15.88}
    for name, (base, spread) in spreads.items():
        noise = np.random.default_rng([zlib.crc32(name.encode()), seed]).standard_normal(out[name].shape)
        drawn = base * np.exp(spread * noise) if base else spread * noise
        out[name] = __import__('jax').numpy.asarray(drawn.astype(out[name].dtype))
    for name, factor in factors.items():
        out[name] = (out[name] * factor).astype(out[name].dtype)
    return out
```

```python
from contextlib import ExitStack

import concourse.bass as bass
from concourse import mybir

F32 = mybir.dt.float32
F32R = mybir.dt.float32r
ALU = mybir.AluOpType
ACT = mybir.ActivationFunctionType
AX = mybir.AxisListType

P = 128
D = 1024
KT = D // P
TC, TS = 128, 512
T = TC + TS
TT = T // P
HALF = T // 2
GRID = 64
CH = 64
H = 8
E = 8
FT = 11
EPS = 1e-6
UNIT = FT * 2 * P
QK_SCALE = float(P) ** -0.5

U_DN_IN, N_DN_IN = 0, 16
U_DN_OUT, N_DN_OUT = 16, 4
U_FFN, N_FFN = 20, 2
U_SC_IN, N_SC_IN = 52, 12
U_SC_OUT, N_SC_OUT = 64, 4
U_MOE, N_MOE = 68, E
PER_EXPERT = 16
N_MOD = 24
DOWN = [(0, 0, 2), (1, 2, 2), (2, 4, 2), (3, 6, 1), (4, 7, 1)]

C_NORM, C_FINAL, C_CONV, C_COND = 0, 32, 40, 112
C_MODB, C_SCCONV, C_DNNORM = 0, 96, 120
N_PAR1, N_PAR2 = 128, 121

PER_HEAD = dict(raw=32, s_init=32, conv=15, silu=4, sqr=2, ssum=2, rs=2, qn=1, kn=1, tok_t=2, ktok=1, vtok=1,
                hcol=1, trig=2, grow=2, er=2, dm=10, ex=2, em=2, qe=2, gram=1, qk=1, lt=10, intra=2, ke=2,
                ml=12, x0=2, p=12, pcopy=10, xm=8, xtm=10, xup=10, xtup=12,
                ks0=10, vp0=10, vnm0=10, vn0=10, om0=10, dsm0=10, sup0=10, ocp0=10,
                ks1=10, vp1=10, vnm1=10, vn1=10, om1=10, dsm1=10, sup1=10, ocp1=10,
                sz=1, osum=1, osq=1, omm=1, ors=1, hsq=3, onrm=1, head=1, st_out=32)


def build(nc, x_prompt, x_sample, state_fwd, state_bwd, c, c_ctx, norm_w, mod_w, mod_b, dn_w_in, dn_conv,
          dn_a_log, dn_dt_bias, dn_norm, dn_w_out, sc_w_in, sc_conv, sc_w_out, ffn_w13, ffn_w2,
          moe_router, moe_router_b, moe_w13, moe_w2, final_norm, y_prompt, y_sample, new_fwd, new_bwd):
    scratch = nc.dram_tensor("projected", (4 * H, P, T), F32, kind="Internal").ap()
    ctx = ExitStack()
    with ctx:
        def sb(name, shape, dt=F32, stack=ctx):
            return stack.enter_context(nc.sbuf_tensor(name, shape, dt))

        sems = {}

        def sem(name):
            if name not in sems:
                sems[name] = ctx.enter_context(nc.semaphore(name))
            return sems[name]

        xT = sb("xT", [P, KT, T])
        raw = [sb(f"raw{s}", [P, UNIT]) for s in range(2)]
        w_hi = [sb(f"w_hi{s}", [P, UNIT], F32R) for s in range(2)]
        w_lo = [sb(f"w_lo{s}", [P, UNIT], F32R) for s in range(2)]
        same = sb("same", [P, 7, P])
        level = sb("level", [P, 6, P])
        tri = sb("tri", [P, 2, P])
        ones = sb("ones", [P, P])
        eps = sb("eps", [P, 1])
        zero = sb("zero", [P, 1])
        ident = same[:, 0, :]
        col1 = sb("col1", [P, N_PAR1])
        col2 = sb("col2", [P, N_PAR2])
        cond = sb("cond", [P, KT, 2])
        mod = sb("mod", [P, 48, 2])
        alpha = sb("alpha", [P, 2, KT, 2])
        tab = sb("tab", [P, 5, 2, H, TT])
        wab_hi = sb("wab_hi", [P, KT, 4 * H], F32R)
        wab_lo = sb("wab_lo", [P, KT, 4 * H], F32R)
        dtb = sb("dtb", [P, 2 * H])
        alog = sb("alog", [P, 2 * H])
        rtb = sb("rtb", [P, E])
        wrt_hi = sb("wrt_hi", [P, KT, E], F32R)
        wrt_lo = sb("wrt_lo", [P, KT, E], F32R)
        gates = sb("gates", [P, TT, E])
        small = sb("small", [P, 6, TT * 2 * H])

        with ExitStack() as fin:
            yT = sb("yT", [P, KT, T], F32, fin)
        with ExitStack() as dense:
            a_hi = sb("a_hi", [P, KT, T], F32R, dense)
            a_lo = sb("a_lo", [P, KT, T], F32R, dense)
            with ExitStack() as hid:
                act_hi = sb("act_hi", [P, FT, T], F32R, hid)
                act_lo = sb("act_lo", [P, FT, T], F32R, hid)
                sg = sb("sg", [P, T], F32, hid)
                prod = sb("prod", [P, T], F32, hid)
                gbc = sb("gbc", [P, T], F32, hid)
                gdiag = sb("gdiag", [P, TT, P], F32, hid)
            with ExitStack() as nrm:
                xtok = sb("xtok", [P, TT, D], F32, nrm)
                sq = sb("sq", [P, 2, T], F32, nrm)
                ms = sb("ms", [P, T], F32, nrm)
                rstd = sb("rstd", [P, T], F32, nrm)
                hp = sb("hp", [P, 2, T], F32, nrm)
                par1 = sb("par1", [P, P], F32, nrm)
                par2 = sb("par2", [P, P], F32, nrm)
                wab = sb("wab", [P, KT, 4 * H], F32, nrm)
                wrt = sb("wrt", [P, KT, E], F32, nrm)
            with ExitStack() as pj:
                stage = sb("stage", [P, 2, 2, T], F32, pj)
            with ExitStack() as sc:
                cu = sb("cu", [P, KT, T], F32, sc)
                cy = sb("cy", [P, KT, T], F32, sc)
            with ExitStack() as rt:
                sm = sb("sm", [P, 6, TT, E], F32, rt)
                cmp_gt = sb("cmp_gt", [P, TT, E, E], F32, rt)
                cmp_eq = sb("cmp_eq", [P, TT, E, E], F32, rt)
                before = sb("before", [P, E, E], F32, rt)
        with ExitStack() as delta:
            oall = sb("oall", [P, H, T], F32, delta)
            praw = sb("praw", [P, 4, T], F32, delta)
            cv = sb("cv", [P, 3, T], F32, delta)
            zs = sb("zs", [P, T], F32, delta)
            ktok = sb("ktok", [P, TT, P], F32, delta)
            vtok = sb("vtok", [P, TT, P], F32, delta)
            er = sb("er", [P, 2, T], F32, delta)
            ee = sb("ee", [P, 2, TT, P], F32, delta)
            lt = sb("lt", [P, 2, TT, P], F32, delta)
            ml = sb("ml", [P, 2, TT, P], F32, delta)
            xx = sb("xx", [P, 2, TT, P], F32, delta)
            xt = sb("xt", [P, 2, TT, P], F32, delta)
            pp = sb("pp", [P, 2, TT, P], F32, delta)
            it = sb("it", [P, 2, TT, P], F32, delta)
            qe = sb("qe", [P, 2, T], F32, delta)
            st = sb("st", [P, 2, 2, P], F32, delta)
            vp = sb("vp", [P, 2, P], F32, delta)
            vn = sb("vn", [P, 2, P], F32, delta)
            hcol = sb("hcol", [P, 5, 2, TT], F32, delta)
            hconv = sb("hconv", [P, 3, 3], F32, delta)
        ke = praw[:, 0:2, :].rearrange("p a (t d) -> p a t d", t=TT)
        ot = praw[:, 2:4, :]
        ytok = xtok

        psum = ctx.enter_context(nc.psum_tensor("psum", [P, 8, 512], F32))
        psf = psum[:, :, :].rearrange("p b c -> p (b c)")

        def wide(k):
            return psf[:, 1024 * k:1024 * k + T]

        def tiles(ap):
            return ap.rearrange("p (t c) -> p t c", t=TT)

        def halves(b):
            return psum[:, b:b + 2, 0:HALF]

        def two(ap):
            return ap.rearrange("p (a c) -> p a c", a=2)

        SPANS = [(0, TC, 0), (TC, T, 1)]

        block = ctx.enter_context(nc.Block())

        @block.sync
        def _(sp):
            for dst, src in [
                (par1[C_NORM:C_NORM + 32, :], norm_w.rearrange("l n (k p) -> (l n k) p", p=P)),
                (par1[C_FINAL:C_FINAL + 8, :], final_norm.rearrange("(k p) -> k p", p=P)),
                (par1[C_CONV:C_CONV + 72, :], dn_conv.rearrange("o j (k p) -> (o j k) p", p=P)),
                (par1[C_COND:C_COND + 8, :], c_ctx.rearrange("(k p) -> k p", p=P)),
                (par1[C_COND + 8:C_COND + 16, :], c.rearrange("o (k p) -> (o k) p", p=P)),
                (par2[C_SCCONV:C_SCCONV + 24, :], sc_conv.rearrange("o j (k p) -> (o j k) p", p=P)),
                (par2[C_DNNORM:C_DNNORM + 1, :], dn_norm),
                (par2[C_MODB:C_MODB + 48, :], mod_b[0].rearrange("(k p) -> k p", p=P)),
                (par2[C_MODB + 48:C_MODB + 96, :], mod_b[1].rearrange("(k p) -> k p", p=P)),
                (xtok[:, 0, :], x_prompt[0]),
                (xtok[:, 1:TT, :], x_sample[0].rearrange("(t p) d -> p t d", p=P)),
                (wab[:, :, :], dn_w_in[0, :, 4 * D:4 * D + 4 * H].rearrange("(k p) m -> p k m", p=P)),
                (wrt[:, :, :], moe_router[0].rearrange("(k p) m -> p k m", p=P)),
                (dtb[:, :], dn_dt_bias.rearrange("o a h -> o (a h)").broadcast_to([P, 2 * H])),
                (alog[:, :], dn_a_log.rearrange("o a h -> o (a h)").broadcast_to([P, 2 * H])),
                (rtb[:, :], moe_router_b.broadcast_to([P, E])),
            ]:
                sp.dma_start(dst, src).then_inc(sem("params"), 16)

            def load(s, dst_src):
                for dst, src in dst_src:
                    sp.dma_start(dst, src).then_inc(sem(f"loaded{s}"), 16)

            def square_unit(w, u, s):
                dst = raw[s][:, 0:KT * 256].rearrange("p (k m) -> p k m", k=KT)
                src = w.rearrange("(k p) m -> p k m", p=P)[:, :, bass.ds(u * 256, 256)]
                load(s, [(dst[:, 0:4, :], src[:, 0:4, :]), (dst[:, 4:8, :], src[:, 4:8, :])])

            def gated_unit(w, j, s, up):
                dst = raw[s][:, 0:KT * 256].rearrange("p (k g m) -> p k g m", k=KT, g=2)
                src = w.rearrange("(k p) m -> p k m", p=P)
                load(s, [(dst[:, :, 0, :], src[:, :, bass.ds(j * P, P)]),
                         (dst[:, :, 1, :], src[:, :, bass.ds(j * P + up, P)])])

            def down_unit(w, row0, m0, nm, s):
                dst = raw[s][:, 0:FT * nm * P].rearrange("p (k m) -> p k m", k=FT)
                src = w[bass.ds(row0, FT * P), m0 * P:(m0 + nm) * P].rearrange("(k p) m -> p k m", p=P)
                load(s, [(dst[:, 0:6, :], src[:, 0:6, :]), (dst[:, 6:FT, :], src[:, 6:FT, :])])

            def pairs(n, fn, free, base, before):
                for s in range(2):
                    if before is not None:
                        sp.wait_ge(sem(before[0]), before[1] - 1 + s)
                    fn(0, s)
                if n > 1:
                    with sp.Fori(1, n) as i:
                        for s in range(2):
                            sp.wait_ge(sem(free), i * 2 + (base + s - 1))
                            fn(i, s)

            def expert_units(u0, w13, w2, j0, row0, up):
                with sp.Fori(0, 5) as i:
                    for s in range(2):
                        sp.wait_ge(sem("split"), i * 2 + u0 + (s - 1))
                        gated_unit(w13, i * 2 + s + j0, s, up)
                sp.wait_ge(sem("split"), u0 + 9)
                gated_unit(w13, j0 + 10, 0, up)
                for n, m0, nm in DOWN:
                    sp.wait_ge(sem("split"), u0 + 10 + n)
                    down_unit(w2, row0, m0, nm, (11 + n) % 2)

            pairs(12, lambda i, s: square_unit(mod_w[0], i * 2 + s, s), "mod_used", 0, None)
            pairs(8, lambda i, s: square_unit(dn_w_in[0], i * 2 + s, s), "split", U_DN_IN, ("mod_used", 24))
            pairs(2, lambda i, s: square_unit(dn_w_out[0], i * 2 + s, s), "split", U_DN_OUT, ("split", U_DN_OUT))
            with sp.Fori(0, N_FFN) as e:
                expert_units(e * PER_EXPERT + U_FFN, ffn_w13[0], ffn_w2[0], e * FT, e * (FT * P), 2 * FT * P)
            pairs(12, lambda i, s: square_unit(mod_w[1], i * 2 + s, s), "mod_used", 24, ("split", U_SC_IN))
            scw = sc_w_in[0]
            pairs(4, lambda i, s: square_unit(scw[:, D:3 * D], i * 2 + s, s), "split", U_SC_IN, ("mod_used", 48))
            pairs(2, lambda i, s: square_unit(scw[:, 0:D], i * 2 + s, s), "split", U_SC_IN + 8, ("split", U_SC_IN + 8))
            pairs(2, lambda i, s: square_unit(sc_w_out[0], i * 2 + s, s), "split", U_SC_OUT, ("split", U_SC_OUT))
            w13_all = moe_w13[0].rearrange("e k m -> (e k) m")
            w2_all = moe_w2[0].rearrange("e k m -> (e k) m")
            with sp.Fori(0, N_MOE) as e:
                expert_units(e * PER_EXPERT + U_MOE, w13_all[bass.ds(e * D, D), :], w2_all, 0, e * (FT * P), FT * P)
            sp.wait_ge(sem("y_evac"), TT)
            sp.dma_start(y_prompt[0], ytok[:, 0, :]).then_inc(sem("y_out"), 16)
            sp.dma_start(y_sample[0].rearrange("(t p) d -> p t d", p=P), ytok[:, 1:TT, :]).then_inc(sem("y_out"), 16)
            sp.wait_ge(sem("y_out"), 32)

        @block.gpsimd
        def _(pool):
            steps = [0]

            def step(ins):
                steps[0] += 1
                ins.then_inc(sem("mask"), 1)
                pool.wait_ge(sem("mask"), steps[0])

            pool.memset(ones[:, :], 1.0).then_inc(sem("ones"), 1)
            step(pool.memset(same[:, :, :], 1.0))
            for b in range(7):
                n = 2 ** b
                v = same[:, b, :].rearrange("p (a r) -> p a r", r=n)
                step(pool.affine_select(out=v, in_=v, pattern=[[-n, P // n], [0, n]], compare_op=ALU.is_ge,
                                        fill=0.0, base=0, channel_multiplier=1))
                step(pool.affine_select(out=v, in_=v, pattern=[[n, P // n], [0, n]], compare_op=ALU.is_ge,
                                        fill=0.0, base=n - 1, channel_multiplier=-1))
            for l in range(6):
                step(pool.tensor_tensor(level[:, l, :], same[:, l + 1, :], same[:, l, :], ALU.subtract))
            step(pool.affine_select(out=tri[:, 0, :], in_=same[:, 6, :], pattern=[[1, P]], compare_op=ALU.is_ge,
                                    fill=0.0, base=0, channel_multiplier=-1))
            step(pool.affine_select(out=tri[:, 1, :], in_=same[:, 6, :], pattern=[[-1, P]], compare_op=ALU.is_ge,
                                    fill=0.0, base=0, channel_multiplier=1))
            step(pool.memset(zero[:, :], 0.0))
            pool.memset(eps[:, :], EPS).then_inc(sem("masks"), 1)

            def split(u, s, cols, loaded, first=False):
                pool.wait_ge(sem(f"loaded{s}"), loaded)
                if not first:
                    pool.wait_ge(sem("multiplied"), u - 1)
                pool.tensor_tensor(w_hi[s][:, 0:cols], raw[s][:, 0:cols], zero[:, :].broadcast_to([P, cols]), ALU.add)\
                    .then_inc(sem("hi"), 1)
                pool.wait_ge(sem("hi"), u + 1)
                pool.tensor_tensor(w_lo[s][:, 0:cols], raw[s][:, 0:cols], w_hi[s][:, 0:cols].bitcast(F32),
                                   ALU.subtract).then_inc(sem("split"), 1)

            def loads(u, s, offset):
                return (u - s + (offset + 2)) * 16

            def pairs(n, u0, offset):
                with pool.Fori(0, n) as i:
                    for s in range(2):
                        u = i * 2 + (u0 + s)
                        split(u, s, KT * 256, loads(u, s, offset))

            def expert_units(u0, offset):
                with pool.Fori(0, 5) as i:
                    for s in range(2):
                        u = i * 2 + u0 + s
                        split(u, s, KT * 256, loads(u, s, offset))
                split(u0 + 10, 0, KT * 256, loads(u0 + 10, 0, offset))
                for n, m0, nm in DOWN:
                    s = (11 + n) % 2
                    split(u0 + 11 + n, s, FT * nm * P, loads(u0 + 11 + n, s, offset))

            for s in range(2):
                split(s, s, KT * 256, 16 * (N_MOD + 2), first=True)
            pairs(9, U_DN_IN + 2, N_MOD)
            with pool.Fori(0, N_FFN) as e:
                expert_units(e * PER_EXPERT + U_FFN, N_MOD)
            pairs(8, U_SC_IN, 2 * N_MOD)
            with pool.Fori(0, N_MOE) as e:
                expert_units(e * PER_EXPERT + U_MOE, 2 * N_MOD)

        def head_wait(eng, name, h, k):
            eng.wait_ge(sem(name), h * PER_HEAD[name] + k)

        def order(d):
            cc = [(0, 0, 0), (0, 0, 1)]
            ss = [(1, 1 + i // 2, i % 2) for i in range(TS // CH)]
            return cc + ss if d == 0 else cc[::-1] + ss[::-1]

        @block.tensor
        def _(pe):
            def wide_mm(k, lhsT, rhs, name):
                pe.matmul(wide(k)[:, 0:512], lhsT, rhs[:, 0:512], start=True, stop=True)
                pe.matmul(wide(k)[:, 512:T], lhsT, rhs[:, 512:T], start=True, stop=True).then_inc(sem(name), 1)

            def tile_mm(k, lhs, rhs, name):
                for t in range(TT):
                    mm = pe.matmul(wide(k)[:, t * P:(t + 1) * P], lhs(t), rhs(t), start=True, stop=True)
                mm.then_inc(sem(name), 1)

            def unit(u, s, kts, nm, mov_hi, mov_lo, first=False):
                pe.wait_ge(sem("split"), u + 1)
                if not first:
                    pe.wait_ge(sem("evacuated"), u - 1)
                wh = w_hi[s][:, 0:kts * nm * P].rearrange("p (k m c) -> p k m c", k=kts, m=nm)
                wl = w_lo[s][:, 0:kts * nm * P].rearrange("p (k m c) -> p k m c", k=kts, m=nm)
                for m in range(nm):
                    for k in range(kts):
                        for n, (w, v) in enumerate(((wh, mov_hi), (wh, mov_lo), (wl, mov_hi))):
                            for a in range(2):
                                mm = pe.matmul(psum[:, 4 * s + 2 * m + a, 0:HALF], w[:, k, m, :],
                                               v[:, k, a * HALF:(a + 1) * HALF],
                                               start=(k == 0 and n == 0), stop=(k == kts - 1 and n == 2))
                mm.then_inc(sem("multiplied"), 1)

            def square_units(n, u0, mov_hi, mov_lo):
                start = 0
                if u0 == 0:
                    for s in range(2):
                        unit(s, s, KT, 2, mov_hi, mov_lo, first=True)
                    start = 1
                if n > start:
                    with pe.Fori(start, n) as i:
                        for s in range(2):
                            unit(i * 2 + (u0 + s), s, KT, 2, mov_hi, mov_lo)

            def modulation(layer):
                done = 0 if layer == 0 else (N_MOD + U_SC_IN) // 2
                with pe.Fori(0, N_MOD // 2) as i:
                    for s in range(2):
                        pe.wait_ge(sem(f"loaded{s}"), i * 32 + 32 * (done + 1))
                        pe.wait_ge(sem("cond"), 2)
                        w = raw[s][:, 0:KT * 256].rearrange("p (k m) -> p k m", k=KT)
                        for m in range(2):
                            for k in range(KT):
                                mm = pe.matmul(psum[:, 0, bass.ds(i * 8 + (4 * s + 2 * m), 2)],
                                               w[:, k, m * P:(m + 1) * P], cond[:, k, :],
                                               start=(k == 0), stop=(k == KT - 1))
                        mm.then_inc(sem("mod_used"), 1)

            def norm(q):
                for k in range(KT):
                    pe.wait_ge(sem("squared"), KT * q + k + 1)
                    for a in range(2):
                        mm = pe.matmul(psum[:, a, 0:HALF], ones[:, :], sq[:, k % 2, a * HALF:(a + 1) * HALF],
                                       start=(k == 0), stop=(k == KT - 1))
                    mm.then_inc(sem("norm_sum"), 1)

            def head(h):
                W = lambda name, k: head_wait(pe, name, h, k)
                pe.wait_ge(sem("head"), h + 1)
                for i in range(2):
                    W("sqr", i + 1)
                    wide_mm(i, ones[:, :], pp[:, i, :, :].rearrange("p t c -> p (t c)"), "ssum")
                W("kn", 1)
                for t in range(TT):
                    mm = pe.transpose(wide(2)[:, t * P:(t + 1) * P], cv[:, 1, t * P:(t + 1) * P], ident)
                mm.then_inc(sem("tok_t"), 1)
                W("silu", 4)
                for t in range(TT):
                    mm = pe.transpose(wide(3)[:, t * P:(t + 1) * P], cv[:, 2, t * P:(t + 1) * P], ident)
                mm.then_inc(sem("tok_t"), 1)
                for d in range(2):
                    W("rs", 2)
                    W("trig", d + 1)
                    wide_mm(d, ones[:, :], pp[:, d, :, :].rearrange("p t c -> p (t c)"), "grow")
                W("ktok", 1)
                kk = lambda t: cv[:, 1, t * P:(t + 1) * P]
                tile_mm(2, kk, kk, "gram")
                W("qn", 1)
                W("vtok", 1)
                tile_mm(3, kk, lambda t: cv[:, 0, t * P:(t + 1) * P], "qk")
                for l in range(6):
                    for d in range(2):
                        W("ml", 2 * l + d + 1)
                        if l == 0:
                            W("er", 2)
                            W("dm", 10)
                            W("intra", 2)
                            tile_mm(2 * d, lambda t: ml[:, d, t, :], lambda t: ident, "p")
                        else:
                            W("xup", 2 * l - 1 + d)
                            W("xtup", 2 * l - 1 + d)
                            tile_mm(2 * d, lambda t: ml[:, d, t, :], lambda t: xx[:, d, t, :], "p")
                    if l == 0:
                        continue
                    for d in range(2):
                        W("pcopy", 2 * l - 1 + d)
                        if l < 5:
                            tile_mm(2 * d + 1, lambda t: xt[:, d, t, :], lambda t: pp[:, d, t, :], "xm")
                        tile_mm(2 * d, lambda t: pp[:, d, t, :], lambda t: xt[:, d, t, :], "xtm")
                for j in range(10):
                    for d in range(2):
                        kind, t, hh = order(d)[j]
                        R = slice(CH * hh, CH * hh + CH)
                        cols = slice(t * P + CH * hh, t * P + CH * hh + CH)
                        if j == 0:
                            W("xtup", 12)
                            W("xup", 10)
                            W("sz", 1)
                            W("s_init", 32)
                        elif j != 2:
                            W(f"sup{d}", j)
                        if j > 0:
                            W(f"vp{d}", j)
                        pe.matmul(psum[R, 4 * d, 0:P], cv[:, 1, cols], st[:, kind, d, :],
                                  start=True, stop=True).then_inc(sem(f"ks{d}"), 1)
                    for d in range(2):
                        kind, t, hh = order(d)[j]
                        R = slice(CH * hh, CH * hh + CH)
                        W(f"vp{d}", j + 1)
                        if j > 0:
                            W(f"vn{d}", j)
                        pe.matmul(psum[:, 4 * d + 1, 0:P], xt[R, d, t, :], vp[R, d, :],
                                  start=True, stop=True).then_inc(sem(f"vnm{d}"), 1)
                    for d in range(2):
                        kind, t, hh = order(d)[j]
                        R = slice(CH * hh, CH * hh + CH)
                        cols = slice(t * P + CH * hh, t * P + CH * hh + CH)
                        W(f"vn{d}", j + 1)
                        W(f"ke", 2)
                        if j > 0:
                            W(f"sup{d}", j)
                            W(f"ocp{d}", j)
                        pe.matmul(psum[:, 4 * d + 3, 0:P], ke[R, d, t, :], vn[R, d, :],
                                  start=True, stop=True).then_inc(sem(f"dsm{d}"), 1)
                        pe.matmul(psum[:, 4 * d + 2, 0:CH], st[:, kind, d, :], qe[:, d, cols], start=True, stop=False)
                        pe.matmul(psum[:, 4 * d + 2, 0:CH], vn[R, d, :], it[R, d, t, R],
                                  start=False, stop=True).then_inc(sem(f"om{d}"), 1)
                W("osq", 1)
                wide_mm(0, ones[:, :], pp[:, 0, :, :].rearrange("p t c -> p (t c)"), "omm")

            def expert(u0, hidden, weighted):
                with pe.Fori(0, 5) as i:
                    for s in range(2):
                        unit(i * 2 + u0 + s, s, KT, 2, a_hi, a_lo)
                if weighted is not None:
                    pe.wait_ge(sem("gdiag"), weighted + 1)
                    pe.wait_ge(sem("evacuated"), u0 + 9)
                    g = gdiag[:, :, :].rearrange("p t c -> p (t c)")
                    pe.matmul(wide(0)[:, 0:512], ones[:, :], g[:, 0:512], start=True, stop=True)
                    pe.matmul(wide(0)[:, 512:T], ones[:, :], g[:, 512:T], start=True, stop=True)\
                        .then_inc(sem("gate_mm"), 1)
                    pe.wait_ge(sem("gate_row"), weighted + 1)
                unit(u0 + 10, 0, KT, 2, a_hi, a_lo)
                for n, m0, nm in DOWN:
                    if n == 0:
                        pe.wait_ge(sem("act_lo"), hidden + (FT + 1))
                    unit(u0 + 11 + n, (11 + n) % 2, FT, nm, act_hi, act_lo)

            pe.wait_ge(sem("params"), 16 * 16)
            pe.wait_ge(sem("masks"), 1)
            pe.wait_ge(sem("ones"), 1)
            pe.transpose(psum[:, 6, 0:N_PAR1], par1[:, :], ident)
            pe.transpose(psum[:, 7, 0:N_PAR2], par2[0:N_PAR2, :], same[0:N_PAR2, 0, 0:N_PAR2])\
                .then_inc(sem("cols_t"), 1)
            for t in range(TT):
                if t >= 2:
                    pe.wait_ge(sem("x_evac"), t - 1)
                for k in range(KT):
                    mm = pe.transpose(psum[:, 2 + 2 * (t % 2) + k // 4, (k % 4) * P:(k % 4 + 1) * P],
                                      xtok[:, t, k * P:(k + 1) * P], ident)
                mm.then_inc(sem("x_t"), 1)
            pe.wait_ge(sem("cond"), 2)
            modulation(0)
            pe.wait_ge(sem("mod_evac"), 1)
            norm(0)
            pe.wait_ge(sem("h_lo"), KT)
            pe.wait_ge(sem("h_hi"), 2 * KT)
            pe.wait_ge(sem("x_evac"), TT)
            square_units(8, U_DN_IN, a_hi, a_lo)
            pe.wait_ge(sem("wab_lo"), 1)
            pe.wait_ge(sem("evacuated"), N_DN_IN)
            for t in range(TT):
                for k in range(KT):
                    for n, (x_, w_) in enumerate(((a_hi, wab_hi), (a_hi, wab_lo), (a_lo, wab_hi))):
                        mm = pe.matmul(psum[:, 0, t * 32:(t + 1) * 32], x_[:, k, t * P:(t + 1) * P], w_[:, k, :],
                                       start=(k == 0 and n == 0), stop=(k == KT - 1 and n == 2))
            mm.then_inc(sem("ab_mm"), 1)
            pe.wait_ge(sem("g_ready"), 1)
            for d in range(2):
                pe.matmul(psum[:, 2, 40 * d:40 * d + 40], tri[:, d, :],
                          tab[:, 0, d, :, :].rearrange("p h t -> p (h t)"), start=True, stop=True)
            pe.matmul(psum[:, 3, 0:80], same[:, 6, :], tab[:, 0, :, :, :].rearrange("p d h t -> p (d h t)"),
                      start=True, stop=True).then_inc(sem("gc_mm"), 1)
            pe.wait_ge(sem("tab"), 3)
            with pe.Fori(0, H) as h:
                head(h)
            pe.wait_ge(sem("head"), H + 1)
            pe.wait_ge(sem("act_lo"), 1)
            square_units(2, U_DN_OUT, act_hi, act_lo)
            norm(1)
            pe.wait_ge(sem("h_lo"), 2 * KT)
            with pe.Fori(0, N_FFN) as e:
                expert(e * PER_EXPERT + U_FFN, e * FT, None)
            pe.wait_ge(sem("evacuated"), U_SC_IN)
            modulation(1)
            pe.wait_ge(sem("mod_evac"), 2)
            norm(2)
            pe.wait_ge(sem("h_lo"), 3 * KT)
            square_units(6, U_SC_IN, a_hi, a_lo)
            pe.wait_ge(sem("cy_split"), 2)
            square_units(2, U_SC_OUT, a_hi, a_lo)
            norm(3)
            pe.wait_ge(sem("h_lo"), 4 * KT)
            pe.wait_ge(sem("wrt_lo"), 1)
            for t in range(TT):
                for k in range(KT):
                    for n, (x_, w_) in enumerate(((a_hi, wrt_hi), (a_hi, wrt_lo), (a_lo, wrt_hi))):
                        mm = pe.matmul(psum[:, 2, t * E:(t + 1) * E], x_[:, k, t * P:(t + 1) * P], w_[:, k, :],
                                       start=(k == 0 and n == 0), stop=(k == KT - 1 and n == 2))
            mm.then_inc(sem("router_mm"), 1)
            pe.wait_ge(sem("rt"), 1)
            with pe.Fori(0, N_MOE) as e:
                expert(e * PER_EXPERT + U_MOE, e * FT + N_FFN * FT, e)
            norm(4)
            for t in range(TT):
                if t == 0:
                    pe.wait_ge(sem("y_scaled"), 2 * KT)
                if t >= 2:
                    pe.wait_ge(sem("y_evac"), t - 1)
                for k in range(KT):
                    mm = pe.transpose(psum[:, 2 + 2 * (t % 2) + k // 4, (k % 4) * P:(k % 4 + 1) * P],
                                      yT[:, k, t * P:(t + 1) * P], ident)
                mm.then_inc(sem("y_t"), 1)

        @block.scalar
        def _(act):
            def norm(q, ready, count):
                act.wait_ge(sem(ready), count)
                for k in range(KT):
                    if k >= 2:
                        act.wait_ge(sem("norm_sum"), KT * q + k - 1)
                    act.activation(sq[:, k % 2, :], xT[:, k, :], ACT.Square).then_inc(sem("squared"), 1)
                act.wait_ge(sem("norm_sum"), KT * (q + 1))
                act.activation(two(ms[:, :]), halves(0), ACT.Sqrt, scale=1.0 / D, bias=eps[:, :])\
                    .then_inc(sem("rms"), 1)

            def norm_hi(q, n):
                for k in range(KT):
                    for i, (c0, c1, w) in enumerate(SPANS):
                        act.wait_ge(sem("h_scaled"), 2 * (KT * q + k) + i + 1)
                        act.activation(a_hi[:, k, c0:c1], hp[:, k % 2, c0:c1], ACT.Identity,
                                       bias=mod[:, 24 * n + k, w:w + 1]).then_inc(sem("h_hi"), 1)

            def evac_stage(u, i, s):
                act.wait_ge(sem("multiplied"), u + 1)
                if i is not None:
                    act.wait_ge(sem(f"stored{s}"), i * 16)
                act.activation(stage[:, s, :, :].rearrange("p m (a c) -> p (m a) c", a=2),
                               psum[:, 4 * s:4 * s + 4, 0:HALF], ACT.Copy).then_inc(sem("evacuated"), 1)
                act.wait_ge(sem("evacuated"), u + 1)
                act.dma_start(scratch.rearrange("(u m) p t -> u p m t", m=2)[bass.ds(u, 1)]
                              .rearrange("o p m t -> p (o m) t"), stage[:, s, :, :]).then_inc(sem(f"stored{s}"), 16)

            def head(h):
                W = lambda name, k: head_wait(act, name, h, k)
                act.wait_ge(sem("head"), h + 1)
                act.dma_start(praw[:, :, :], scratch.rearrange("(g h) p t -> h p g t", g=4)[bass.ds(h, 1)]
                              .rearrange("o p g t -> p (o g) t")).then_inc(sem("raw"), 32)
                for d, src in enumerate((state_fwd, state_bwd)):
                    act.dma_start(st[:, 1, d, :], src[0, 0, bass.ds(h, 1)].rearrange("o k v -> (o k) v"))\
                        .then_inc(sem("s_init"), 16)
                W("raw", 32)
                act.activation(zs[:, :], praw[:, 3, :], ACT.Silu).then_inc(sem("silu"), 1)
                for i in (0, 1, 2):
                    W("conv", 5 * (i + 1))
                    act.activation(cv[:, i, :], cv[:, i, :], ACT.Silu).then_inc(sem("silu"), 1)
                for i in range(2):
                    W("silu", i + 2)
                    act.activation(pp[:, i, :, :].rearrange("p t c -> p (t c)"), cv[:, i, :], ACT.Square)\
                        .then_inc(sem("sqr"), 1)
                for i in range(2):
                    W("ssum", i + 1)
                    act.activation(er[:, i, :], wide(i), ACT.Sqrt, bias=eps[:, :]).then_inc(sem("hsq"), 1)
                W("tok_t", 1)
                act.activation(ktok[:, :, :], tiles(wide(2)), ACT.Copy).then_inc(sem("ktok"), 1)
                W("tok_t", 2)
                act.activation(vtok[:, :, :], tiles(wide(3)), ACT.Copy).then_inc(sem("vtok"), 1)
                W("qn", 1)
                W("kn", 1)
                for d in range(2):
                    W("grow", d + 1)
                    W("dm", 5 * d + 5)
                    act.activation(er[:, d, :], wide(d), ACT.Exp).then_inc(sem("er"), 1)
                    act.activation(ee[:, d, :, :], ee[:, d, :, :], ACT.Exp).then_inc(sem("ex"), 1)
                for l in range(1, 6):
                    for d in range(2):
                        W("p", 2 * l + d + 1)
                        act.activation(pp[:, d, :, :], tiles(wide(2 * d)), ACT.Copy).then_inc(sem("pcopy"), 1)
                for j in range(10):
                    for d in range(2):
                        kind, t, hh = order(d)[j]
                        R = slice(CH * hh, CH * hh + CH)
                        W(f"vnm{d}", j + 1)
                        if j > 0:
                            W(f"om{d}", j)
                        act.activation(vn[R, d, :], psum[R, 4 * d + 1, 0:P], ACT.Copy,
                                       scale=hcol[R, 1, d, t:t + 1]).then_inc(sem(f"vn{d}"), 1)
                    for d in range(2):
                        kind, t, hh = order(d)[j]
                        cols = slice(t * P + CH * hh, t * P + CH * hh + CH)
                        W(f"om{d}", j + 1)
                        act.activation(ot[:, d, cols], psum[:, 4 * d + 2, 0:CH], ACT.Copy).then_inc(sem(f"ocp{d}"), 1)
                for d, dst in enumerate((new_fwd, new_bwd)):
                    W(f"sup{d}", 2)
                    act.dma_start(dst[0, 0, bass.ds(h, 1)].rearrange("o k v -> (o k) v"), st[:, 0, d, :])\
                        .then_inc(sem("st_out"), 16)
                W("st_out", 32)
                W("osum", 1)
                act.activation(pp[:, 0, :, :].rearrange("p t c -> p (t c)"), ot[:, 0, :], ACT.Square)\
                    .then_inc(sem("osq"), 1)
                W("omm", 1)
                act.activation(er[:, 0, :], wide(0), ACT.Sqrt, scale=1.0 / P, bias=eps[:, :]).then_inc(sem("hsq"), 1)

            def gate_unit(u, s, j):
                act.wait_ge(sem("multiplied"), u + 1)
                act.wait_ge(sem("evacuated"), u)
                act.activation(two(sg[:, :]), halves(4 * s), ACT.Silu).then_inc(sem("silu_g"), 1)
                act.wait_ge(sem("evacuated"), u + 1)
                act.activation(act_hi[:, bass.ds(j, 1), :].rearrange("p o c -> p (o c)"), prod[:, :],
                               ACT.Copy).then_inc(sem("act_hi"), 1)

            def expert(u0, weighted):
                with act.Fori(0, 5) as i:
                    for s in range(2):
                        gate_unit(i * 2 + u0 + s, s, i * 2 + s)
                if weighted is not None:
                    act.wait_ge(sem("gate_mm"), weighted + 1)
                    act.activation(gbc[:, :], wide(0), ACT.Copy).then_inc(sem("gate_row"), 1)
                gate_unit(u0 + 10, 0, FT - 1)

            act.wait_ge(sem("masks"), 1)
            act.wait_ge(sem("ones"), 1)
            act.wait_ge(sem("cols"), 1)
            for w in range(2):
                act.activation(cond[:, :, w], col1[:, C_COND + 8 * w:C_COND + 8 * w + 8], ACT.Silu)\
                    .then_inc(sem("cond"), 1)
            act.wait_ge(sem("params"), 16 * 16)
            act.activation(wab_hi[:, :, :], wab[:, :, :], ACT.Copy).then_inc(sem("wab_hi"), 1)
            act.activation(wrt_hi[:, :, :], wrt[:, :, :], ACT.Copy).then_inc(sem("wrt_hi"), 1)
            norm(0, "x_evac", TT)
            act.wait_ge(sem("alpha"), 2)
            norm_hi(0, 0)
            for s in range(2):
                evac_stage(s, None, s)
            with act.Fori(1, N_DN_IN // 2) as i:
                for s in range(2):
                    evac_stage(i * 2 + s, i, s)
            act.wait_ge(sem("negabs"), 1)
            act.activation(small[:, 1, :], small[:, 1, :], ACT.Exp).then_inc(sem("e_negabs"), 1)
            act.wait_ge(sem("e_negabs"), 1)
            act.activation(small[:, 1, :], small[:, 1, :], ACT.Ln, bias=ones[:, 0:1]).then_inc(sem("ln1p"), 1)
            act.activation(alog[:, :], alog[:, :], ACT.Exp).then_inc(sem("ea"), 1)
            act.wait_ge(sem("ab_mm"), 1)
            act.wait_ge(sem("ab_read"), 1)
            act.activation(small[:, 3, :].rearrange("p (t c) -> p t c", t=TT),
                           psum[:, 0, 0:160].rearrange("p (t c) -> p t c", t=TT)[:, :, 16:32], ACT.Exp,
                           scale=-1.0).then_inc(sem("e_b"), 1)
            act.wait_ge(sem("gc"), 1)
            act.activation(small[:, 4, :], small[:, 4, :], ACT.Exp).then_inc(sem("e_gc"), 1)
            act.wait_ge(sem("gdiff"), 1)
            act.activation(tab[:, 4, :, :, :].rearrange("p d h t -> p (d h t)"), small[:, 5, :], ACT.Exp)\
                .then_inc(sem("tab"), 1)
            act.wait_ge(sem("stored0"), 16 * 8)
            act.wait_ge(sem("stored1"), 16 * 8)
            act.wait_ge(sem("tab"), 3)
            with act.Fori(0, H) as h:
                head(h)
            act.wait_ge(sem("head"), H + 1)
            act.activation(act_hi[:, 0:H, :], oall[:, :, :], ACT.Copy).then_inc(sem("o_hi"), 1)
            norm(1, "evacuated", U_FFN)
            norm_hi(1, 1)
            with act.Fori(0, N_FFN) as e:
                expert(e * PER_EXPERT + U_FFN, None)
            norm(2, "evacuated", U_SC_IN)
            act.wait_ge(sem("alpha"), 4)
            norm_hi(2, 0)
            with act.Fori(0, 2) as i:
                for s in range(2):
                    u = i * 2 + (U_SC_IN + s)
                    act.wait_ge(sem("multiplied"), u + 1)
                    act.activation(cu[:, bass.ds(i * 4 + 2 * s, 2), :].rearrange("p m (a c) -> p (m a) c", a=2),
                                   psum[:, 4 * s:4 * s + 4, 0:HALF], ACT.Copy).then_inc(sem("evacuated"), 1)
            act.wait_ge(sem("evacuated"), U_SC_IN + N_SC_IN)
            act.activation(a_hi[:, :, :], cy[:, :, :], ACT.Copy).then_inc(sem("cy_hi"), 1)
            norm(3, "evacuated", U_MOE)
            norm_hi(3, 1)
            act.wait_ge(sem("rt_shift"), 1)
            act.activation(sm[:, 1, :, :], sm[:, 1, :, :], ACT.Exp).then_inc(sem("rt_exp"), 1)
            with act.Fori(0, N_MOE) as e:
                expert(e * PER_EXPERT + U_MOE, e)
            norm(4, "evacuated", U_MOE + N_MOE * PER_EXPERT)

        @block.vector
        def _(dve):
            def norm(q, w_of, out=None):
                dve.wait_ge(sem("rms"), q + 1)
                dve.reciprocal(rstd[:, :], ms[:, :]).then_inc(sem("rstd"), 1)
                dve.wait_ge(sem("rstd"), q + 1)
                n = q % 2

                def scaled(k):
                    if out is None and k >= 2:
                        dve.wait_ge(sem("h_lo"), KT * q + k - 1)
                    for c0, c1, w in SPANS:
                        dst = hp[:, k % 2, c0:c1] if out is None else out[:, k, c0:c1]
                        dve.scalar_tensor_tensor(out=dst, in0=xT[:, k, c0:c1], scalar=w_of(k, w), in1=rstd[:, c0:c1],
                                                 op0=ALU.mult, op1=ALU.mult)\
                            .then_inc(sem("h_scaled" if out is None else "y_scaled"), 1)

                def rest(k):
                    for i, (c0, c1, w) in enumerate(SPANS):
                        dve.wait_ge(sem("h_hi"), 2 * (KT * q + k) + i + 1)
                        ins = dve.scalar_tensor_tensor(out=a_lo[:, k, c0:c1], in0=hp[:, k % 2, c0:c1],
                                                       scalar=mod[:, 24 * n + k, w:w + 1],
                                                       in1=a_hi[:, k, c0:c1].bitcast(F32),
                                                       op0=ALU.add, op1=ALU.subtract)
                    ins.then_inc(sem("h_lo"), 1)

                scaled(0)
                if out is None:
                    for k in range(KT):
                        if k + 1 < KT:
                            scaled(k + 1)
                        rest(k)
                else:
                    for k in range(1, KT):
                        scaled(k)

            def modulation(layer):
                dve.wait_ge(sem("mod_used"), N_MOD * (layer + 1))
                b = col2[:, C_MODB + 48 * layer:C_MODB + 48 * layer + 48].unsqueeze(2).broadcast_to([P, 48, 2])
                dve.tensor_tensor(mod[:, :, :], psum[:, 0, 0:96].rearrange("p (m w) -> p m w", w=2), b, ALU.add)\
                    .then_inc(sem("mod_evac"), 1)
                dve.wait_ge(sem("mod_evac"), layer + 1)
                for n in range(2):
                    nw = col1[:, C_NORM + 16 * layer + 8 * n:C_NORM + 16 * layer + 8 * n + 8]\
                        .unsqueeze(2).broadcast_to([P, KT, 2])
                    dve.scalar_tensor_tensor(out=alpha[:, n, :, :], in0=mod[:, 24 * n + 8:24 * n + 16, :], scalar=1.0,
                                             in1=nw, op0=ALU.add, op1=ALU.mult).then_inc(sem("alpha"), 1)
                dve.wait_ge(sem("alpha"), 2 * layer + 2)

            def a_of(n):
                return lambda k, w: alpha[:, n, k, w:w + 1]

            PIECES = [(0, 0, TC, 0), (0, TC, HALF - TC, 1), (1, 0, HALF, 1)]

            def residual(u, s, m_of, nm, gmod, last=None):
                dve.wait_ge(sem("multiplied"), u + 1)
                for m in range(nm):
                    for b, c0, n, w in PIECES:
                        xs = xT[:, bass.ds(m_of + m, 1), b * HALF + c0:b * HALF + c0 + n]\
                            .rearrange("p o c -> p (o c)")
                        ins = dve.scalar_tensor_tensor(out=xs, in0=psum[:, 4 * s + 2 * m + b, c0:c0 + n],
                                                       scalar=mod[:, bass.ds(m_of + (gmod + m), 1), w], in1=xs,
                                                       op0=ALU.mult, op1=ALU.add)
                ins.then_inc(sem("evacuated"), 1)

            def out_units(u0, gmod):
                with dve.Fori(0, 2) as i:
                    for s in range(2):
                        residual(i * 2 + (u0 + s), s, i * 4 + 2 * s, 2, gmod)

            def gate_unit(u, s, j, n0):
                dve.wait_ge(sem("silu_g"), n0 + 1)
                dve.wait_ge(sem("act_lo"), n0 + 1)
                dve.tensor_tensor(two(prod[:, :]), two(sg[:, :]), halves(4 * s + 2), ALU.mult)\
                    .then_inc(sem("evacuated"), 1)
                dve.wait_ge(sem("act_hi"), n0 + 1)
                dve.tensor_tensor(act_lo[:, bass.ds(j, 1), :].rearrange("p o c -> p (o c)"), prod[:, :],
                                  act_hi[:, bass.ds(j, 1), :].rearrange("p o c -> p (o c)").bitcast(F32),
                                  ALU.subtract).then_inc(sem("act_lo"), 1)

            def expert(u0, n0, weighted):
                if weighted is not None:
                    gb = gates[:, :, bass.ds(weighted, 1)].broadcast_to([P, TT, P])
                    dve.tensor_tensor(gdiag[:, :, :], ident.unsqueeze(1).broadcast_to([P, TT, P]), gb, ALU.mult)\
                        .then_inc(sem("gdiag"), 1)
                with dve.Fori(0, 5) as i:
                    for s in range(2):
                        gate_unit(i * 2 + u0 + s, s, i * 2 + s, i * 2 + n0 + s)
                gate_unit(u0 + 10, 0, FT - 1, n0 + 10)
                for n, m0, nm in DOWN:
                    u, s = u0 + 11 + n, (11 + n) % 2
                    if weighted is None:
                        dve.wait_ge(sem("evacuated"), u)
                        dve.wait_ge(sem("multiplied"), u + 1)
                        for m in range(nm):
                            for b, c0, w_, w in PIECES:
                                xs = xT[:, m0 + m, b * HALF + c0:b * HALF + c0 + w_]
                                ins = dve.scalar_tensor_tensor(out=xs, in0=psum[:, 4 * s + 2 * m + b, c0:c0 + w_],
                                                               scalar=mod[:, 40 + m0 + m, w:w + 1], in1=xs,
                                                               op0=ALU.mult, op1=ALU.add)
                        ins.then_inc(sem("evacuated"), 1)
                    else:
                        dve.wait_ge(sem("multiplied"), u + 1)
                        for m in range(nm):
                            if m == 0:
                                dve.wait_ge(sem("evacuated"), u)
                            else:
                                dve.wait_ge(sem("x_added"), weighted * 3 + (n + 1))
                            for b, c0, w_, w in PIECES:
                                r = slice(b * HALF + c0, b * HALF + c0 + w_)
                                ins = dve.scalar_tensor_tensor(out=prod[:, r], in0=psum[:, 4 * s + 2 * m + b, c0:c0 + w_],
                                                               scalar=mod[:, 40 + m0 + m, w:w + 1], in1=gbc[:, r],
                                                               op0=ALU.mult, op1=ALU.mult)
                            ins.then_inc(sem("y_gated"), 1)
                            dve.wait_ge(sem("y_gated"), weighted * 8 + (m0 + m + 1))
                            dve.tensor_tensor(xT[:, m0 + m, :], xT[:, m0 + m, :], prod[:, :], ALU.add)\
                                .then_inc(sem("evacuated" if m == nm - 1 else "x_added"), 1)

            def conv(dst, src, w, tag, n0):
                def lat(ap):
                    return ap[:, TC:T].rearrange("p (r c) -> p r c", c=GRID)
                dve.tensor_scalar(dst, src, w(1), None, ALU.mult).then_inc(sem(tag), 1)
                dve.wait_ge(sem(tag), n0 + 1)
                taps = [(dst[:, 1:TC], src[:, 0:TC - 1], w(0)),
                        (lat(dst)[:, :, 1:GRID], lat(src)[:, :, 0:GRID - 1], w(0)),
                        (dst[:, 0:TC - 1], src[:, 1:TC], w(2)),
                        (lat(dst)[:, :, 0:GRID - 1], lat(src)[:, :, 1:GRID], w(2))]
                for i, (o_, i_, wt) in enumerate(taps):
                    if i == 2:
                        dve.wait_ge(sem(tag), n0 + 3)
                    dve.scalar_tensor_tensor(out=o_, in0=i_, scalar=wt, in1=o_, op0=ALU.mult, op1=ALU.add)\
                        .then_inc(sem(tag), 1)

            def head(h):
                W = lambda name, k: head_wait(dve, name, h, k)
                dve.tensor_copy(hcol[:, :, :, :].rearrange("p q d t -> p (q d) t"),
                                tab[:, :, :, bass.ds(h, 1), :].rearrange("p q d o t -> p (q d) (o t)"))\
                    .then_inc(sem("hcol"), 1)
                dve.tensor_copy(hconv[:, :, :],
                                col1[:, C_CONV:C_CONV + 72].rearrange("p (j i h) -> p j i h", j=3, i=3)
                                [:, :, :, bass.ds(h, 1)].rearrange("p j i o -> p j (i o)")).then_inc(sem("hconv"), 1)
                dve.memset(st[:, 0, :, :], 0.0).then_inc(sem("sz"), 1)
                W("hcol", 1)
                dve.wait_ge(sem("hconv"), h + 1)
                W("raw", 32)
                for i in range(3):
                    conv(cv[:, i, :], praw[:, i, :], lambda j: hconv[:, j, i:i + 1], "conv",
                         h * PER_HEAD["conv"] + 5 * i)
                for i, (nm, sc) in enumerate((("qn", QK_SCALE), ("kn", 1.0))):
                    W("hsq", i + 1)
                    dve.reciprocal(er[:, i, :], er[:, i, :]).then_inc(sem("rs"), 1)
                    W("rs", i + 1)
                    W("silu", i + 2)
                    dve.scalar_tensor_tensor(out=cv[:, i, :], in0=cv[:, i, :], scalar=sc, in1=er[:, i, :],
                                             op0=ALU.mult, op1=ALU.mult).then_inc(sem(nm), 1)
                for d in range(2):
                    W("ssum", 2)
                    dve.tensor_tensor(pp[:, d, :, :], tri[:, d, :].unsqueeze(1).broadcast_to([P, TT, P]),
                                      hcol[:, 0, d, :].unsqueeze(2).broadcast_to([P, TT, P]), ALU.mult)\
                        .then_inc(sem("trig"), 1)
                for d in range(2):
                    W("grow", d + 1)
                    for t in range(TT):
                        dve.tensor_scalar(ee[:, d, t, :], wide(d)[:, t * P:(t + 1) * P], hcol[:, 2, d, t:t + 1], 0.0,
                                          ALU.subtract, ALU.min).then_inc(sem("dm"), 1)
                for d in range(2):
                    W("ex", d + 1)
                    dve.tensor_tensor(ee[:, d, :, :], ee[:, d, :, :],
                                      tri[:, d, :].unsqueeze(1).broadcast_to([P, TT, P]), ALU.mult)\
                        .then_inc(sem("em"), 1)
                W("gram", 1)
                for d in range(2):
                    W("em", d + 1)
                    for t in range(TT):
                        dve.scalar_tensor_tensor(out=lt[:, d, t, :], in0=wide(2)[:, t * P:(t + 1) * P],
                                                 scalar=hcol[:, 1, d, t:t + 1], in1=ee[:, d, t, :],
                                                 op0=ALU.mult, op1=ALU.mult).then_inc(sem("lt"), 1)

                def masked(l, d):
                    if l > 0:
                        W("p", 2 * l - 1 + d)
                    if l == 1:
                        W("xtup", d + 1)
                    dve.tensor_tensor(ml[:, d, :, :], lt[:, d, :, :],
                                      level[:, l, :].unsqueeze(1).broadcast_to([P, TT, P]), ALU.mult)\
                        .then_inc(sem("ml"), 1)

                idb = ident.unsqueeze(1).broadcast_to([P, TT, P])
                for d in range(2):
                    W("lt", 5 * d + 5)
                    masked(0, d)
                W("qk", 1)
                for d in range(2):
                    dve.tensor_tensor(it[:, d, :, :], tiles(wide(3)), ee[:, d, :, :], ALU.mult)\
                        .then_inc(sem("intra"), 1)
                for d in range(2):
                    W("er", d + 1)
                    W("qn", 1)
                    dve.tensor_tensor(qe[:, d, :], cv[:, 0, :], er[:, d, :], ALU.mult).then_inc(sem("qe"), 1)
                W("ktok", 1)
                W("silu", 4)
                for d in range(2):
                    dve.tensor_tensor(ke[:, d, :, :], ktok[:, :, :],
                                      hcol[:, 4, d, :].unsqueeze(2).broadcast_to([P, TT, P]), ALU.mult)\
                        .then_inc(sem("ke"), 1)
                for d in range(2):
                    W("ml", d + 1)
                    dve.tensor_tensor(xt[:, d, :, :], idb, ml[:, d, :, :], ALU.subtract).then_inc(sem("xtup"), 1)
                    W("p", d + 1)
                    dve.tensor_tensor(xx[:, d, :, :], idb, tiles(wide(2 * d)), ALU.subtract).then_inc(sem("xup"), 1)
                for d in range(2):
                    masked(1, d)
                for l in range(1, 6):
                    for d in range(2):
                        W("xtm", 2 * (l - 1) + d + 1)
                        if l < 5:
                            W("xm", 2 * (l - 1) + d + 1)
                            W("xup", 2 * l - 1 + d)
                            dve.tensor_tensor(xx[:, d, :, :], xx[:, d, :, :], tiles(wide(2 * d + 1)), ALU.subtract)\
                                .then_inc(sem("xup"), 1)
                        W("xtup", 2 * l - 1 + d)
                        dve.tensor_tensor(xt[:, d, :, :], xt[:, d, :, :], tiles(wide(2 * d)), ALU.subtract)\
                            .then_inc(sem("xtup"), 1)
                        if l < 5:
                            masked(l + 1, d)
                for j in range(10):
                    for d in range(2):
                        kind, t, hh = order(d)[j]
                        R = slice(CH * hh, CH * hh + CH)
                        W(f"ks{d}", j + 1)
                        W("vtok", 1)
                        if j > 0:
                            W(f"vnm{d}", j)
                        dve.scalar_tensor_tensor(out=vp[R, d, :], in0=psum[R, 4 * d, 0:P],
                                                 scalar=hcol[R, 3, d, t:t + 1], in1=vtok[R, t, :],
                                                 op0=ALU.mult, op1=ALU.add).then_inc(sem(f"vp{d}"), 1)
                    for d in range(2):
                        kind, t, hh = order(d)[j]
                        last = t * P + CH * hh + (CH - 1 if d == 0 else 0)
                        W(f"om{d}", j + 1)
                        if j > 0:
                            W(f"sup{d}", j)
                        dve.scalar_tensor_tensor(out=st[:, kind, d, :], in0=st[:, kind, d, :],
                                                 scalar=er[:, d, last:last + 1], in1=psum[:, 4 * d + 3, 0:P],
                                                 op0=ALU.mult, op1=ALU.add).then_inc(sem(f"sup{d}"), 1)
                W("ocp0", 10)
                W("ocp1", 10)
                dve.tensor_tensor(ot[:, 0, :], ot[:, 0, :], ot[:, 1, :], ALU.add).then_inc(sem("osum"), 1)
                W("hsq", 3)
                dve.reciprocal(er[:, 0, :], er[:, 0, :]).then_inc(sem("ors"), 1)
                W("ors", 1)
                dve.scalar_tensor_tensor(out=er[:, 1, :], in0=ot[:, 0, :],
                                         scalar=col2[:, C_DNNORM:C_DNNORM + 1], in1=er[:, 0, :],
                                         op0=ALU.mult, op1=ALU.mult).then_inc(sem("onrm"), 1)
                W("onrm", 1)
                dve.tensor_tensor(oall[:, bass.ds(h, 1), :].rearrange("p o c -> p (o c)"), er[:, 1, :], zs[:, :],
                                  ALU.mult).then_inc(sem("head"), 1)
                dve.wait_ge(sem("head"), h + 2)

            dve.wait_ge(sem("cols_t"), 1)
            dve.tensor_copy(col1[:, :], psum[:, 6, 0:N_PAR1]).then_inc(sem("col1"), 1)
            dve.tensor_copy(col2[:, :], psum[:, 7, 0:N_PAR2]).then_inc(sem("cols"), 1)
            dve.wait_ge(sem("cols"), 1)
            for t in range(TT):
                dve.wait_ge(sem("x_t"), t + 1)
                b = 2 + 2 * (t % 2)
                dve.tensor_copy(xT[:, :, t * P:(t + 1) * P],
                                psum[:, b:b + 2, :].rearrange("p b (k c) -> p (b k) c", c=P)).then_inc(sem("x_evac"), 1)
            dve.wait_ge(sem("x_evac"), TT)
            for hi, lo, w, tag in ((wab_hi, wab_lo, wab, "wab"), (wrt_hi, wrt_lo, wrt, "wrt")):
                dve.wait_ge(sem(tag + "_hi"), 1)
                dve.tensor_tensor(lo[:, :, :], w[:, :, :], hi[:, :, :].bitcast(F32), ALU.subtract)\
                    .then_inc(sem(tag + "_lo"), 1)
            modulation(0)
            norm(0, a_of(0))
            dve.wait_ge(sem("ab_mm"), 1)
            ab = psum[:, 0, 0:160].rearrange("p (t c) -> p t c", t=TT)
            tv = lambda i: small[:, i, :].rearrange("p (t c) -> p t c", t=TT)
            dve.tensor_tensor(tv(0), ab[:, :, 0:16], dtb[:, :].unsqueeze(1).broadcast_to([P, TT, 2 * H]), ALU.add)\
                .then_inc(sem("ab_read"), 1)
            dve.wait_ge(sem("ab_read"), 1)
            dve.tensor_scalar(small[:, 1, :], small[:, 0, :], -1.0, None, ALU.mult).then_inc(sem("neg"), 1)
            dve.tensor_scalar(small[:, 2, :], small[:, 0, :], 0.0, None, ALU.max).then_inc(sem("pos"), 1)
            dve.wait_ge(sem("neg"), 1)
            dve.tensor_tensor(small[:, 1, :], small[:, 1, :], small[:, 0, :], ALU.min).then_inc(sem("negabs"), 1)
            dve.wait_ge(sem("ln1p"), 1)
            dve.wait_ge(sem("pos"), 1)
            dve.tensor_tensor(small[:, 2, :], small[:, 2, :], small[:, 1, :], ALU.add).then_inc(sem("softplus"), 1)
            dve.wait_ge(sem("softplus"), 1)
            dve.wait_ge(sem("ea"), 1)
            dve.scalar_tensor_tensor(out=tv(0), in0=tv(2), scalar=-1.0,
                                     in1=alog[:, :].unsqueeze(1).broadcast_to([P, TT, 2 * H]),
                                     op0=ALU.mult, op1=ALU.mult).then_inc(sem("g_tok"), 1)
            dve.wait_ge(sem("g_tok"), 1)
            dve.tensor_copy(tab[:, 0, :, :, :].rearrange("p d h t -> p (d h) t"),
                            tv(0).rearrange("p t c -> p c t")).then_inc(sem("g_ready"), 1)
            dve.wait_ge(sem("e_b"), 1)
            dve.tensor_scalar(small[:, 3, :], small[:, 3, :], 1.0, None, ALU.add).then_inc(sem("b1"), 1)
            dve.wait_ge(sem("b1"), 1)
            dve.reciprocal(small[:, 3, :], small[:, 3, :]).then_inc(sem("b2"), 1)
            dve.wait_ge(sem("b2"), 1)
            dve.tensor_copy(tab[:, 1, :, :, :].rearrange("p d h t -> p (d h) t"),
                            tv(3).rearrange("p t c -> p c t")).then_inc(sem("tab"), 1)
            dve.wait_ge(sem("gc_mm"), 1)
            gcol = tab[:, 2, :, :, :].rearrange("p d h t -> p (d h t)")
            dve.tensor_copy(gcol, psum[:, 2, 0:80]).then_inc(sem("gcol"), 1)
            dve.wait_ge(sem("gcol"), 1)
            dve.tensor_copy(small[:, 4, :], gcol).then_inc(sem("gc"), 1)
            dve.tensor_tensor(small[:, 5, :], psum[:, 3, 0:80], gcol, ALU.subtract).then_inc(sem("gdiff"), 1)
            dve.wait_ge(sem("e_gc"), 1)
            dve.tensor_scalar(tab[:, 3, :, :, :].rearrange("p d h t -> p (d h t)"), small[:, 4, :], -1.0, None,
                              ALU.mult).then_inc(sem("tab"), 1)
            dve.wait_ge(sem("tab"), 3)
            dve.memset(st[:, 0, :, :], 0.0).then_inc(sem("head"), 1)
            dve.wait_ge(sem("head"), 1)
            with dve.Fori(0, H) as h:
                head(h)
            dve.wait_ge(sem("o_hi"), 1)
            dve.tensor_tensor(act_lo[:, 0:H, :], oall[:, :, :], act_hi[:, 0:H, :].bitcast(F32), ALU.subtract)\
                .then_inc(sem("act_lo"), 1)
            out_units(U_DN_OUT, 16)
            norm(1, a_of(1))
            with dve.Fori(0, N_FFN) as e:
                expert(e * PER_EXPERT + U_FFN, e * FT, None)
            modulation(1)
            norm(2, a_of(0))
            with dve.Fori(0, 2) as i:
                for s in range(2):
                    u = i * 2 + (U_SC_IN + 4 + s)
                    dve.wait_ge(sem("multiplied"), u + 1)
                    dve.wait_ge(sem("evacuated"), U_SC_IN + 4)
                    v = cu[:, bass.ds(i * 4 + 2 * s, 2), :].rearrange("p m (a c) -> p (m a) c", a=2)
                    dve.tensor_tensor(v, v, psum[:, 4 * s:4 * s + 4, 0:HALF], ALU.mult).then_inc(sem("evacuated"), 1)
            dve.wait_ge(sem("evacuated"), U_SC_IN + 8)
            for k in range(KT):
                conv(cy[:, k, :], cu[:, k, :],
                     lambda j: col2[:, C_SCCONV + 8 * j + k:C_SCCONV + 8 * j + k + 1], "sconv", 5 * k)
            dve.wait_ge(sem("sconv"), 5 * KT)
            with dve.Fori(0, 2) as i:
                for s in range(2):
                    u = i * 2 + (U_SC_IN + 8 + s)
                    dve.wait_ge(sem("multiplied"), u + 1)
                    v = cy[:, bass.ds(i * 4 + 2 * s, 2), :].rearrange("p m (a c) -> p (m a) c", a=2)
                    dve.tensor_tensor(v, v, psum[:, 4 * s:4 * s + 4, 0:HALF], ALU.mult).then_inc(sem("evacuated"), 1)
            dve.wait_ge(sem("cy_hi"), 1)
            dve.tensor_tensor(a_lo[:, :, :], cy[:, :, :], a_hi[:, :, :].bitcast(F32), ALU.subtract)\
                .then_inc(sem("cy_split"), 2)
            out_units(U_SC_OUT, 16)
            norm(3, a_of(1))
            dve.wait_ge(sem("router_mm"), 1)
            rt = [0]

            def step(ins):
                rt[0] += 1
                ins.then_inc(sem("rt"), 1)
                dve.wait_ge(sem("rt"), rt[0])

            lg = sm[:, 0, :, :]
            red = lambda i: sm[:, 5, :, i:i + 1]
            wideE = lambda ap: ap.broadcast_to([P, TT, E])
            step(dve.tensor_tensor(lg, psum[:, 2, 0:TT * E].rearrange("p (t e) -> p t e", e=E),
                                   rtb[:, :].unsqueeze(1).broadcast_to([P, TT, E]), ALU.add))
            step(dve.tensor_reduce(red(0).rearrange("p t o -> p (t o)"), lg, AX.X, ALU.max))
            dve.tensor_tensor(sm[:, 1, :, :], lg, wideE(red(0)), ALU.subtract).then_inc(sem("rt_shift"), 1)
            dve.wait_ge(sem("rt_exp"), 1)
            step(dve.tensor_reduce(red(1).rearrange("p t o -> p (t o)"), sm[:, 1, :, :], AX.X, ALU.add))
            step(dve.reciprocal(red(2), red(1)))
            step(dve.tensor_tensor(sm[:, 2, :, :], sm[:, 1, :, :], wideE(red(2)), ALU.mult))
            pe_ = sm[:, 2, :, :].unsqueeze(3).broadcast_to([P, TT, E, E])
            pf_ = sm[:, 2, :, :].unsqueeze(2).broadcast_to([P, TT, E, E])
            step(dve.memset(before[:, :, :], 0.0))
            for e in range(1, E):
                step(dve.memset(before[:, e, 0:e], 1.0))
            for t in range(TT):
                step(dve.tensor_tensor(cmp_gt[:, t], pf_[:, t], pe_[:, t], ALU.is_gt))
                step(dve.tensor_tensor(cmp_eq[:, t], pf_[:, t], pe_[:, t], ALU.is_equal))
            step(dve.tensor_tensor(cmp_eq[:, :, :, :].rearrange("p t e f -> p t (e f)"),
                                   cmp_eq[:, :, :, :].rearrange("p t e f -> p t (e f)"),
                                   before[:, :, :].rearrange("p e f -> p (e f)").unsqueeze(1)
                                   .broadcast_to([P, TT, E * E]), ALU.mult))
            step(dve.tensor_tensor(cmp_gt[:, :, :, :], cmp_gt[:, :, :, :], cmp_eq[:, :, :, :], ALU.add))
            step(dve.tensor_reduce(sm[:, 3, :, :].rearrange("p t e -> p (t e)"),
                                   cmp_gt[:, :, :, :].rearrange("p t e f -> p (t e) f"), AX.X, ALU.add))
            step(dve.scalar_tensor_tensor(out=sm[:, 4, :, :], in0=sm[:, 3, :, :], scalar=2.0, in1=sm[:, 2, :, :],
                                          op0=ALU.is_lt, op1=ALU.mult))
            step(dve.tensor_reduce(red(3).rearrange("p t o -> p (t o)"), sm[:, 4, :, :], AX.X, ALU.add))
            step(dve.reciprocal(red(4), red(3)))
            step(dve.tensor_tensor(gates[:, :, :], sm[:, 4, :, :], wideE(red(4)), ALU.mult))
            with dve.Fori(0, N_MOE) as e:
                expert(e * PER_EXPERT + U_MOE, e * FT + N_FFN * FT, e)
            norm(4, lambda k, w: col1[:, C_FINAL + k:C_FINAL + k + 1], out=yT)
            for t in range(TT):
                dve.wait_ge(sem("y_t"), t + 1)
                b = 2 + 2 * (t % 2)
                dve.tensor_copy(ytok[:, t, :].rearrange("p (k c) -> p k c", c=P),
                                psum[:, b:b + 2, :].rearrange("p b (k c) -> p (b k) c", c=P)).then_inc(sem("y_evac"), 1)


_INS = ['x_prompt', 'x_sample', 'state_fwd', 'state_bwd', 'c', 'c_ctx', 'norm_w', 'mod_w', 'mod_b', 'dn_w_in',
        'dn_conv', 'dn_a_log', 'dn_dt_bias', 'dn_norm', 'dn_w_out', 'sc_w_in', 'sc_conv', 'sc_w_out', 'ffn_w13',
        'ffn_w2', 'moe_router', 'moe_router_b', 'moe_w13', 'moe_w2', 'final_norm']
_OUTS = [((1, 128, 1024), 'float32'), ((1, 512, 1024), 'float32'),
         ((1, 1, 8, 128, 128), 'float32'), ((1, 1, 8, 128, 128), 'float32')]


def kernel(**inputs):
    import numpy as _np
    import concourse.bacc as _bacc
    from concourse import mybir as _mybir
    from concourse.bass_utils import run_bass_kernel_spmd as _run

    nc = _bacc.Bacc("TRN2", target_bir_lowering=False, num_devices=1)
    arrays, args = {}, []
    for name in _INS:
        a = _np.ascontiguousarray(inputs[name])
        arrays[f"in_{name}_dram"] = a
        args.append(nc.dram_tensor(f"in_{name}_dram", a.shape, _mybir.dt.from_np(a.dtype), kind="ExternalInput").ap())
    for i, (shape, dtype) in enumerate(_OUTS):
        dt = _mybir.dt.from_np(_np.dtype(dtype))
        args.append(nc.dram_tensor(f"out_{i}_dram", shape, dt, kind="ExternalOutput").ap())
    build(nc, *args)
    r = _run(nc, [arrays], core_ids=[0])
    return tuple(r.results[0][f"out_{i}_dram"] for i in range(len(_OUTS)))
```

```python
from contextlib import ExitStack

import concourse.bass as bass
from concourse import mybir

F32 = mybir.dt.float32
F32R = mybir.dt.float32r
ALU = mybir.AluOpType
ACT = mybir.ActivationFunctionType
AX = mybir.AxisListType

P = 128
D = 1024
KT = D // P
TC, TS = 128, 512
T = TC + TS
TT = T // P
HALF = T // 2
GRID = 64
CH = 64
H = 8
E = 8
FT = 11
EPS = 1e-6
UNIT = FT * 2 * P
QK_SCALE = float(P) ** -0.5

U_DN_IN, N_DN_IN = 0, 16
U_DN_OUT, N_DN_OUT = 16, 4
U_FFN, N_FFN = 20, 2
U_SC_IN, N_SC_IN = 52, 12
U_SC_OUT, N_SC_OUT = 64, 4
U_MOE = 68
PER_EXPERT = 16

CAP = 192
SLOTS = [(0, 0, P), (1, P, CAP - P)]
MAX_PASS = -(-T // CAP)
MAX_ITEMS = E + 2 * T // CAP
FAR = 4096.0
DOWN_K = [(0, 2), (2, 2), (4, 2), (6, 2), (8, 1), (9, 1), (10, 1)]
M_UNITS = FT + len(DOWN_K)
M_UNIT = KT * 2 * P
N_MOD = 24
N_SLOT = 6
MOD_PER_HEAD = 6
MOD_COL = 400
DOWN = [(0, 0, 2), (1, 2, 2), (2, 4, 2), (3, 6, 1), (4, 7, 1)]

C_NORM, C_FINAL, C_CONV, C_COND = 0, 32, 40, 112
C_MODB, C_SCCONV, C_DNNORM = 0, 96, 120
N_PAR1, N_PAR2 = 128, 121

PER_HEAD = dict(raw=32, s_init=32, conv=15, silu=4, sqr=2, ssum=2, rs=2, qn=1, kn=1, tok_t=2, ktok=1, vtok=1,
                hcol=2, trig=2, grow=2, er=2, dm=10, ex=2, em=2, qe=2, gram=1, qk=1, lt=10, intra=2, ke=2,
                ml=12, x0=2, p=12, pcopy=10, xm=8, xtm=10, xup=10, xtup=12,
                ks0=10, vp0=10, vnm0=10, vn0=10, om0=10, dsm0=10, sup0=10, ocp0=10,
                ks1=10, vp1=10, vnm1=10, vn1=10, om1=10, dsm1=10, sup1=10, ocp1=10,
                sz=1, osum=1, osq=1, omm=1, ors=1, hsq=3, onrm=1, head=1, st_out=32)


def build(nc, x_prompt, x_sample, state_fwd, state_bwd, c, c_ctx, norm_w, mod_w, mod_b, dn_w_in, dn_conv,
          dn_a_log, dn_dt_bias, dn_norm, dn_w_out, sc_w_in, sc_conv, sc_w_out, ffn_w13, ffn_w2,
          moe_router, moe_router_b, moe_w13, moe_w2, final_norm, y_prompt, y_sample, new_fwd, new_bwd):
    scratch = nc.dram_tensor("projected", (4 * H, P, T), F32, kind="Internal").ap()
    ctx = ExitStack()
    with ctx:
        def sb(name, shape, dt=F32, stack=ctx):
            return stack.enter_context(nc.sbuf_tensor(name, shape, dt))

        sems = {}

        def sem(name):
            if name not in sems:
                sems[name] = ctx.enter_context(nc.semaphore(name))
            return sems[name]

        xT = sb("xT", [P, KT, T])
        same = sb("same", [P, 7, P])
        level = sb("level", [P, 6, P])
        earlier = sb("earlier", [P, P])
        tri = sb("tri", [P, 2, P])
        ones = sb("ones", [P, P])
        eps = sb("eps", [P, 1])
        zero = sb("zero", [P, 1])
        ident = same[:, 0, :]
        col1 = sb("col1", [P, N_PAR1])
        col2 = sb("col2", [P, N_PAR2])
        cond = sb("cond", [P, KT, 2])
        mod = sb("mod", [P, 48, 2])
        alpha = sb("alpha", [P, 2, KT, 2])
        tab = sb("tab", [P, 5, 2, H, TT])
        wab_hi = sb("wab_hi", [P, KT, 4 * H], F32R)
        wab_lo = sb("wab_lo", [P, KT, 4 * H], F32R)
        dtb = sb("dtb", [P, 2 * H])
        alog = sb("alog", [P, 2 * H])
        rtb = sb("rtb", [P, E])
        wrt_hi = sb("wrt_hi", [P, KT, E], F32R)
        wrt_lo = sb("wrt_lo", [P, KT, E], F32R)
        gates = sb("gates", [P, TT, E])
        g_now = sb("g_now", [P, TT])
        items = sb("items", [P, MAX_ITEMS + 2], mybir.dt.int32)
        slots = sb("slots", [P, CAP])
        small = sb("small", [P, 6, TT * 2 * H])

        weights = ExitStack()
        raw = [sb(f"raw{s}", [P, UNIT], F32, weights) for s in range(2)]
        w_hi = [sb(f"w_hi{s}", [P, UNIT], F32R, weights) for s in range(2)]
        w_lo = [sb(f"w_lo{s}", [P, UNIT], F32R, weights) for s in range(2)]

        with ExitStack() as early:
            m_slot = raw + [sb(f"mod_raw{i}", [P, KT * 256], F32, early) for i in range(4)]
        with ExitStack() as fin:
            yT = sb("yT", [P, KT, T], F32, fin)
        with ExitStack() as dense:
            a_hi = sb("a_hi", [P, KT, T], F32R, dense)
            a_lo = sb("a_lo", [P, KT, T], F32R, dense)
            with ExitStack() as hid:
                act_hi = sb("act_hi", [P, FT, T], F32R, hid)
                act_lo = sb("act_lo", [P, FT, T], F32R, hid)
                sg = sb("sg", [P, T], F32, hid)
                prod = sb("prod", [P, T], F32, hid)
            with ExitStack() as nrm:
                xtok = sb("xtok", [P, TT, D], F32, nrm)
                sq = sb("sq", [P, 2, T], F32, nrm)
                ms = sb("ms", [P, T], F32, nrm)
                rstd = sb("rstd", [P, T], F32, nrm)
                hp = sb("hp", [P, 2, T], F32, nrm)
                par1 = sb("par1", [P, P], F32, nrm)
                par2 = sb("par2", [P, P], F32, nrm)
                wab = sb("wab", [P, KT, 4 * H], F32, nrm)
                wrt = sb("wrt", [P, KT, E], F32, nrm)
            with ExitStack() as pj:
                stage = sb("stage", [P, 2, 2, T], F32, pj)
            with ExitStack() as sc:
                cu = sb("cu", [P, KT, T], F32, sc)
                cy = sb("cy", [P, KT, T], F32, sc)
            with ExitStack() as rt:
                sb("rt_gap", [P, 2 * FT * T], F32, rt)
                sm = sb("sm", [P, 6, TT, E], F32, rt)
                cmp_gt = sb("cmp_gt", [P, TT, E, E], F32, rt)
                cmp_eq = sb("cmp_eq", [P, TT, E, E], F32, rt)
                before = sb("before", [P, E, E], F32, rt)
                sel = sb("sel", [P, TT, E], F32, rt)
                cum = sb("cum", [P, TT + 1, E], F32, rt)
                slot_of = sb("slot_of", [P, TT, E], F32, rt)
                n_of = sb("n_of", [P, 2, E], F32, rt)
                first = sb("first", [P, E + 1], F32, rt)
                nth = sb("nth", [P, MAX_ITEMS + 1, E], F32, rt)
                mine = sb("mine", [P, MAX_ITEMS + 1, E], F32, rt)
                picked = sb("picked", [P, MAX_ITEMS + 1, E], F32, rt)
                item_e = sb("item_e", [P, MAX_ITEMS + 1], F32, rt)
        with ExitStack() as delta:
            oall = sb("oall", [P, H, T], F32, delta)
            praw = sb("praw", [P, 4, T], F32, delta)
            ke = sb("ke", [P, 2, TT, P], F32, delta)
            ot = sb("ot", [P, 2, T], F32, delta)
            cv = sb("cv", [P, 3, T], F32, delta)
            zs = sb("zs", [P, T], F32, delta)
            ktok = sb("ktok", [P, TT, P], F32, delta)
            vtok = sb("vtok", [P, TT, P], F32, delta)
            er = sb("er", [P, 2, T], F32, delta)
            ee = sb("ee", [P, 2, TT, P], F32, delta)
            lt = sb("lt", [P, 2, TT, P], F32, delta)
            ml = sb("ml", [P, 2, TT, P], F32, delta)
            xx = sb("xx", [P, 2, TT, P], F32, delta)
            xt = sb("xt", [P, 2, TT, P], F32, delta)
            pp = sb("pp", [P, 2, TT, P], F32, delta)
            it = sb("it", [P, 2, TT, P], F32, delta)
            qe = sb("qe", [P, 2, T], F32, delta)
            st = sb("st", [P, 2, 2, P], F32, delta)
            vp = sb("vp", [P, 2, P], F32, delta)
            vn = sb("vn", [P, 2, P], F32, delta)
            hcol = sb("hcol", [P, 5, 2, TT], F32, delta)
            hconv = sb("hconv", [P, 3, 3], F32, delta)
        weights.close()
        with ExitStack() as moe:
            m_raw = [sb(f"m_raw{s}", [P, M_UNIT], F32, moe) for s in range(2)]
            m_hi = [sb(f"m_hi{s}", [P, M_UNIT], F32R, moe) for s in range(3)]
            m_lo = [sb(f"m_lo{s}", [P, M_UNIT], F32R, moe) for s in range(3)]
            sb("m_gap", [P, 6 * UNIT - 8 * M_UNIT], F32, moe)
            he_hi = sb("he_hi", [P, KT, CAP], F32R, moe)
            he_lo = sb("he_lo", [P, KT, CAP], F32R, moe)
            hid_hi = sb("hid_hi", [P, FT, CAP], F32R, moe)
            hid_lo = sb("hid_lo", [P, FT, CAP], F32R, moe)
            m_sg = sb("m_sg", [P, CAP], F32, moe)
            m_prod = sb("m_prod", [P, CAP], F32, moe)
            pick = sb("pick", [P, TT, CAP], F32R, moe)
            item_slot = sb("item_slot", [P, TT, MAX_ITEMS + 1], F32, moe)
            item_gate = sb("item_gate", [P, TT, MAX_ITEMS + 1], F32, moe)
            sb("m_gap2", [P, 2 * KT * T - (2 * KT + 2 * FT + 2 + TT) * CAP - 2 * TT * (MAX_ITEMS + 1)], F32, moe)
            ht_hi = sb("ht_hi", [P, TT, D], F32R, moe)
            ht_lo = sb("ht_lo", [P, TT, D], F32R, moe)
            y_hi = sb("y_hi", [P, 2, D], F32R, moe)
            y_lo = sb("y_lo", [P, 2, D], F32R, moe)
            back = sb("back", [P, 2, T], F32R, moe)
            g_slot = sb("g_slot", [P, 2], F32, moe)
        ytok = xtok

        psum = ctx.enter_context(nc.psum_tensor("psum", [P, 8, 512], F32))
        psf = psum[:, :, :].rearrange("p b c -> p (b c)")

        def wide(k):
            return psf[:, 1024 * k:1024 * k + T]

        def tiles(ap):
            return ap.rearrange("p (t c) -> p t c", t=TT)

        def halves(b):
            return psum[:, b:b + 2, 0:HALF]

        def two(ap):
            return ap.rearrange("p (a c) -> p a c", a=2)

        SPANS = [(0, TC, 0), (TC, T, 1)]

        block = ctx.enter_context(nc.Block())

        @block.sync
        def _(sp):
            for dst, src in [
                (par1[C_NORM:C_NORM + 32, :], norm_w.rearrange("l n (k p) -> (l n k) p", p=P)),
                (par1[C_FINAL:C_FINAL + 8, :], final_norm.rearrange("(k p) -> k p", p=P)),
                (par1[C_CONV:C_CONV + 72, :], dn_conv.rearrange("o j (k p) -> (o j k) p", p=P)),
                (par1[C_COND:C_COND + 8, :], c_ctx.rearrange("(k p) -> k p", p=P)),
                (par1[C_COND + 8:C_COND + 16, :], c.rearrange("o (k p) -> (o k) p", p=P)),
                (par2[C_SCCONV:C_SCCONV + 24, :], sc_conv.rearrange("o j (k p) -> (o j k) p", p=P)),
                (par2[C_DNNORM:C_DNNORM + 1, :], dn_norm),
                (par2[C_MODB:C_MODB + 48, :], mod_b[0].rearrange("(k p) -> k p", p=P)),
                (par2[C_MODB + 48:C_MODB + 96, :], mod_b[1].rearrange("(k p) -> k p", p=P)),
                (xtok[:, 0, :], x_prompt[0]),
                (xtok[:, 1:TT, :], x_sample[0].rearrange("(t p) d -> p t d", p=P)),
                (wab[:, :, :], dn_w_in[0, :, 4 * D:4 * D + 4 * H].rearrange("(k p) m -> p k m", p=P)),
                (wrt[:, :, :], moe_router[0].rearrange("(k p) m -> p k m", p=P)),
                (dtb[:, :], dn_dt_bias.rearrange("o a h -> o (a h)").broadcast_to([P, 2 * H])),
                (alog[:, :], dn_a_log.rearrange("o a h -> o (a h)").broadcast_to([P, 2 * H])),
                (rtb[:, :], moe_router_b.broadcast_to([P, E])),
            ]:
                sp.dma_start(dst, src).then_inc(sem("params"), 16)

            def load(s, dst_src):
                for dst, src in dst_src:
                    sp.dma_start(dst, src).then_inc(sem(f"loaded{s}"), 16)

            def square_unit(w, u, s):
                dst = raw[s][:, 0:KT * 256].rearrange("p (k m) -> p k m", k=KT)
                src = w.rearrange("(k p) m -> p k m", p=P)[:, :, bass.ds(u * 256, 256)]
                load(s, [(dst[:, 0:4, :], src[:, 0:4, :]), (dst[:, 4:8, :], src[:, 4:8, :])])

            def gated_unit(w, j, s, up):
                dst = raw[s][:, 0:KT * 256].rearrange("p (k g m) -> p k g m", k=KT, g=2)
                src = w.rearrange("(k p) m -> p k m", p=P)
                load(s, [(dst[:, :, 0, :], src[:, :, bass.ds(j * P, P)]),
                         (dst[:, :, 1, :], src[:, :, bass.ds(j * P + up, P)])])

            def down_unit(w, row0, m0, nm, s):
                dst = raw[s][:, 0:FT * nm * P].rearrange("p (k m) -> p k m", k=FT)
                src = w[bass.ds(row0, FT * P), m0 * P:(m0 + nm) * P].rearrange("(k p) m -> p k m", p=P)
                load(s, [(dst[:, 0:6, :], src[:, 0:6, :]), (dst[:, 6:FT, :], src[:, 6:FT, :])])

            def pairs(n, fn, free, base, before):
                for s in range(2):
                    if before is not None:
                        sp.wait_ge(sem(before[0]), before[1] - 1 + s)
                    fn(0, s)
                if n > 1:
                    with sp.Fori(1, n) as i:
                        for s in range(2):
                            sp.wait_ge(sem(free), i * 2 + (base + s - 1))
                            fn(i, s)

            def expert_units(u0, w13, w2, j0, row0, up):
                with sp.Fori(0, 5) as i:
                    for s in range(2):
                        sp.wait_ge(sem("split"), i * 2 + u0 + (s - 1))
                        gated_unit(w13, i * 2 + s + j0, s, up)
                sp.wait_ge(sem("split"), u0 + 9)
                gated_unit(w13, j0 + 10, 0, up)
                for n, m0, nm in DOWN:
                    sp.wait_ge(sem("split"), u0 + 10 + n)
                    down_unit(w2, row0, m0, nm, (11 + n) % 2)

            def mod_unit(i, s):
                dst = m_slot[s][:, 0:KT * 256].rearrange("p (k m) -> p k m", k=KT)
                src = mod_w[0].rearrange("(k p) m -> p k m", p=P)[:, :, bass.ds(i * (N_SLOT * 256) + s * 256, 256)]
                sp.dma_start(dst, src).then_inc(sem(f"mod_in{s}"), 16)

            for s in range(N_SLOT):
                mod_unit(0, s)
            with sp.Fori(1, N_MOD // N_SLOT) as i:
                for s in range(N_SLOT):
                    sp.wait_ge(sem("mod_used"), i * N_SLOT + (s + 1 - N_SLOT))
                    mod_unit(i, s)
            pairs(8, lambda i, s: square_unit(dn_w_in[0], i * 2 + s, s), "split", U_DN_IN, ("mod_used", N_MOD))
            sp.wait_ge(sem("split"), U_DN_OUT)
            with sp.Fori(0, H) as h:
                for i in range(MOD_PER_HEAD):
                    sp.wait_ge(sem("mod_used"), h * MOD_PER_HEAD + (N_MOD + i - 1))
                    sp.dma_start(raw[i % 2][:, 0:KT * P].rearrange("p (k m) -> p k m", k=KT),
                                 mod_w[1].rearrange("(k p) m -> p k m", p=P)
                                 [:, :, bass.ds(h * (MOD_PER_HEAD * P) + i * P, P)])\
                        .then_inc(sem(f"loaded{i % 2}"), 16)
            pairs(2, lambda i, s: square_unit(dn_w_out[0], i * 2 + s, s), "split", U_DN_OUT,
                  ("mod_used", N_MOD + H * MOD_PER_HEAD))
            with sp.Fori(0, N_FFN) as e:
                expert_units(e * PER_EXPERT + U_FFN, ffn_w13[0], ffn_w2[0], e * FT, e * (FT * P), 2 * FT * P)
            scw = sc_w_in[0]
            pairs(4, lambda i, s: square_unit(scw[:, D:3 * D], i * 2 + s, s), "split", U_SC_IN, ("split", U_SC_IN))
            pairs(2, lambda i, s: square_unit(scw[:, 0:D], i * 2 + s, s), "split", U_SC_IN + 8, ("split", U_SC_IN + 8))
            pairs(2, lambda i, s: square_unit(sc_w_out[0], i * 2 + s, s), "split", U_SC_OUT, ("split", U_SC_OUT))
            w13_all = moe_w13[0].rearrange("e k m -> (e k) m")
            w2_all = moe_w2[0].rearrange("e k m -> (e k) m")

            def m_load(j, turn, dst_src):
                sp.wait_ge(sem(f"m_split{j % 2}"), turn + (j // 2 + 1))
                for dst, src in dst_src:
                    sp.dma_start(dst, src).then_inc(sem(f"m_loaded{j % 2}"), 16)

            sp.wait_ge(sem("items"), 1)
            n_items = sp.value_load(items[0:1, MAX_ITEMS + 1:MAX_ITEMS + 2], min_val=1, max_val=MAX_ITEMS)

            def m_gated(x, tiles_):
                e = sp.value_load(items[0:1, bass.ds(x, 1)], min_val=0, max_val=E - 1)
                turn = x * (M_UNITS // 2)
                src13 = w13_all[bass.ds(e * D, D), :].rearrange("(k p) m -> p k m", p=P)
                for j in tiles_:
                    dst = m_raw[j % 2][:, :].rearrange("p (k g m) -> p k g m", k=KT, g=2)
                    m_load(j, turn, [(dst[:, :, g, :], src13[:, :, (g * FT + j) * P:(g * FT + j + 1) * P])
                                     for g in range(2)])
                return e, turn

            with sp.Fori(0, n_items) as x:
                e, turn = m_gated(x, range(FT))
                src2 = w2_all[bass.ds(e * (FT * P), FT * P), :].rearrange("(k p) m -> p k m", p=P)
                for n, (k0, nk) in enumerate(DOWN_K):
                    j = FT + n
                    dst = m_raw[j % 2][:, 0:nk * D].rearrange("p (k m) -> p k m", k=nk)
                    m_load(j, turn, [(dst[:, :, 512 * g:512 * g + 512], src2[:, k0:k0 + nk, 512 * g:512 * g + 512])
                                     for g in range(2)])
            m_gated(n_items, range(2))
            sp.wait_ge(sem("y_evac"), TT)
            sp.dma_start(y_prompt[0], ytok[:, 0, :]).then_inc(sem("y_out"), 16)
            sp.dma_start(y_sample[0].rearrange("(t p) d -> p t d", p=P), ytok[:, 1:TT, :]).then_inc(sem("y_out"), 16)
            sp.wait_ge(sem("y_out"), 32)

        def head_wait(eng, name, h, k):
            eng.wait_ge(sem(name), h * PER_HEAD[name] + k)

        def m_cols(j):
            return M_UNIT if j < FT else DOWN_K[j - FT][1] * D

        def m_low(eng, x, j):
            n, q = m_cols(j), j % 3
            eng.wait_ge(sem("m_high"), x * M_UNITS + (j + 1))
            eng.tensor_tensor(m_lo[q][:, 0:n], m_raw[j % 2][:, 0:n], m_hi[q][:, 0:n].bitcast(F32), ALU.subtract)\
            .then_inc(sem(f"m_split{j % 2}"), 1)

        @block.gpsimd
        def _(pool):
            steps = [0]

            def step(ins):
                steps[0] += 1
                ins.then_inc(sem("mask"), 1)
                pool.wait_ge(sem("mask"), steps[0])

            pool.iota(slots[:, :], pattern=[[1, CAP]], base=0, channel_multiplier=0,
                      allow_small_or_imprecise_dtypes=True).then_inc(sem("slots"), 1)
            pool.memset(ones[:, :], 1.0).then_inc(sem("ones"), 1)
            pool.wait_ge(sem("ones"), 1)
            step(pool.memset(same[:, :, :], 1.0))
            for b in range(7):
                n = 2 ** b
                v = same[:, b, :].rearrange("p (a r) -> p a r", r=n)
                step(pool.affine_select(out=v, in_=v, pattern=[[-n, P // n], [0, n]], compare_op=ALU.is_ge,
                                        fill=0.0, base=0, channel_multiplier=1))
                step(pool.affine_select(out=v, in_=v, pattern=[[n, P // n], [0, n]], compare_op=ALU.is_ge,
                                        fill=0.0, base=n - 1, channel_multiplier=-1))
            for l in range(6):
                step(pool.tensor_tensor(level[:, l, :], same[:, l + 1, :], same[:, l, :], ALU.subtract))
            step(pool.affine_select(out=tri[:, 0, :], in_=same[:, 6, :], pattern=[[1, P]], compare_op=ALU.is_ge,
                                    fill=0.0, base=0, channel_multiplier=-1))
            step(pool.affine_select(out=tri[:, 1, :], in_=same[:, 6, :], pattern=[[-1, P]], compare_op=ALU.is_ge,
                                    fill=0.0, base=0, channel_multiplier=1))
            step(pool.affine_select(out=earlier[:, :], in_=ones[:, :], pattern=[[1, P]], compare_op=ALU.is_gt,
                                    fill=0.0, base=0, channel_multiplier=-1))
            step(pool.memset(zero[:, :], 0.0))
            pool.memset(eps[:, :], EPS).then_inc(sem("masks"), 1)

            def split(u, s, cols, loaded, first=False):
                pool.wait_ge(sem(f"loaded{s}"), loaded)
                if not first:
                    pool.wait_ge(sem("multiplied"), u - 1)
                pool.tensor_tensor(w_hi[s][:, 0:cols], raw[s][:, 0:cols], zero[:, :].broadcast_to([P, cols]), ALU.add)\
                    .then_inc(sem("hi"), 1)
                pool.wait_ge(sem("hi"), u + 1)
                pool.tensor_tensor(w_lo[s][:, 0:cols], raw[s][:, 0:cols], w_hi[s][:, 0:cols].bitcast(F32),
                                   ALU.subtract).then_inc(sem("split"), 1)

            def loads(u, s, offset):
                return (u - s + (offset + 2)) * 16

            def pairs(n, u0, offset):
                with pool.Fori(0, n) as i:
                    for s in range(2):
                        u = i * 2 + (u0 + s)
                        split(u, s, KT * 256, loads(u, s, offset))

            def expert_units(u0, offset):
                with pool.Fori(0, 5) as i:
                    for s in range(2):
                        u = i * 2 + u0 + s
                        split(u, s, KT * 256, loads(u, s, offset))
                split(u0 + 10, 0, KT * 256, loads(u0 + 10, 0, offset))
                for n, m0, nm in DOWN:
                    s = (11 + n) % 2
                    split(u0 + 11 + n, s, FT * nm * P, loads(u0 + 11 + n, s, offset))

            def head_products():
                with pool.Fori(0, H) as h:
                    W = lambda name, k: head_wait(pool, name, h, k)

                    def masked(l):
                        for d in range(2):
                            if l == 1:
                                W("xtup", d + 1)
                            W("p", 2 * l - 1 + d)
                            pool.tensor_tensor(ml[:, d, :, :], lt[:, d, :, :],
                                               level[:, l, :].unsqueeze(1).broadcast_to([P, TT, P]), ALU.mult)\
                                .then_inc(sem("ml"), 1)

                    masked(1)
                    for d in range(2):
                        W("er", 2)
                        W("qn", 1)
                        pool.tensor_tensor(qe[:, d, :], cv[:, 0, :], er[:, d, :], ALU.mult).then_inc(sem("qe"), 1)
                    masked(2)
                    W("ktok", 1)
                    for d in range(2):
                        pool.tensor_tensor(ke[:, d, :, :], ktok[:, :, :],
                                           hcol[:, 4, d, :].unsqueeze(2).broadcast_to([P, TT, P]), ALU.mult)\
                            .then_inc(sem("ke"), 1)
                    for l in (3, 4, 5):
                        masked(l)

            for s in range(2):
                split(s, s, KT * 256, 16 * 2, first=True)
            pairs(7, U_DN_IN + 2, 0)
            head_products()
            pairs(2, U_DN_OUT, N_MOD)
            with pool.Fori(0, N_FFN) as e:
                expert_units(e * PER_EXPERT + U_FFN, N_MOD)
            pairs(8, U_SC_IN, N_MOD)
            pool.wait_ge(sem("items"), 1)
            pool.memset(m_lo[0][:, 0:1].bitcast(F32), 0.0).then_inc(sem("m_split0"), 1)
            pool.memset(back[:, :, :].bitcast(F32), 0.0).then_inc(sem("y_split"), 1)
            for y in (y_hi, y_lo):
                ins = pool.memset(y[:, :, :].bitcast(F32), 0.0)
            ins.then_inc(sem("y_split"), 1)
            n_items = pool.value_load(items[0:1, MAX_ITEMS + 1:MAX_ITEMS + 2], min_val=1, max_val=MAX_ITEMS)
            with pool.Fori(0, n_items) as x:
                for j in range(0, M_UNITS, 2):
                    m_low(pool, x, j)

        def order(d):
            cc = [(0, 0, 0), (0, 0, 1)]
            ss = [(1, 1 + i // 2, i % 2) for i in range(TS // CH)]
            return cc + ss if d == 0 else cc[::-1] + ss[::-1]

        @block.tensor
        def _(pe):
            def wide_mm(k, lhsT, rhs, name):
                pe.matmul(wide(k)[:, 0:512], lhsT, rhs[:, 0:512], start=True, stop=True)
                pe.matmul(wide(k)[:, 512:T], lhsT, rhs[:, 512:T], start=True, stop=True).then_inc(sem(name), 1)

            def tile_mm(k, lhs, rhs, name):
                for t in range(TT):
                    mm = pe.matmul(wide(k)[:, t * P:(t + 1) * P], lhs(t), rhs(t), start=True, stop=True)
                mm.then_inc(sem(name), 1)

            def unit(u, s, kts, nm, mov_hi, mov_lo, first=False):
                pe.wait_ge(sem("split"), u + 1)
                if not first:
                    pe.wait_ge(sem("evacuated"), u - 1)
                wh = w_hi[s][:, 0:kts * nm * P].rearrange("p (k m c) -> p k m c", k=kts, m=nm)
                wl = w_lo[s][:, 0:kts * nm * P].rearrange("p (k m c) -> p k m c", k=kts, m=nm)
                for m in range(nm):
                    for k in range(kts):
                        for n, (w, v) in enumerate(((wh, mov_hi), (wh, mov_lo), (wl, mov_hi))):
                            for a in range(2):
                                mm = pe.matmul(psum[:, 4 * s + 2 * m + a, 0:HALF], w[:, k, m, :],
                                               v[:, k, a * HALF:(a + 1) * HALF],
                                               start=(k == 0 and n == 0), stop=(k == kts - 1 and n == 2))
                mm.then_inc(sem("multiplied"), 1)

            def square_units(n, u0, mov_hi, mov_lo):
                start = 0
                if u0 == 0:
                    for s in range(2):
                        unit(s, s, KT, 2, mov_hi, mov_lo, first=True)
                    start = 1
                if n > start:
                    with pe.Fori(start, n) as i:
                        for s in range(2):
                            unit(i * 2 + (u0 + s), s, KT, 2, mov_hi, mov_lo)

            def modulation():
                pe.wait_ge(sem("cond"), 2)
                with pe.Fori(0, N_MOD // N_SLOT) as i:
                    for s in range(N_SLOT):
                        pe.wait_ge(sem(f"mod_in{s}"), i * 16 + 16)
                        w = m_slot[s][:, 0:KT * 256].rearrange("p (k m) -> p k m", k=KT)
                        for m in range(2):
                            for k in range(KT):
                                mm = pe.matmul(psum[:, 0, bass.ds(i * (4 * N_SLOT) + (4 * s + 2 * m), 2)],
                                               w[:, k, m * P:(m + 1) * P], cond[:, k, :],
                                               start=(k == 0), stop=(k == KT - 1))
                        mm.then_inc(sem("mod_used"), 1)

            def next_modulation(h, tiles_):
                for i in tiles_:
                    pe.wait_ge(sem(f"loaded{i % 2}"),
                               h * (8 * MOD_PER_HEAD) + 16 * (N_DN_IN + i // 2 + 1))
                    w = raw[i % 2][:, 0:KT * P].rearrange("p (k m) -> p k m", k=KT)
                    for k in range(KT):
                        mm = pe.matmul(psum[:, 7, bass.ds(h * (2 * MOD_PER_HEAD) + (MOD_COL + 2 * i), 2)],
                                       w[:, k, :], cond[:, k, :], start=(k == 0), stop=(k == KT - 1))
                    mm.then_inc(sem("mod_used"), 1)

            def norm(q):
                for k in range(KT):
                    pe.wait_ge(sem("squared"), KT * q + k + 1)
                    for a in range(2):
                        mm = pe.matmul(psum[:, a, 0:HALF], ones[:, :], sq[:, k % 2, a * HALF:(a + 1) * HALF],
                                       start=(k == 0), stop=(k == KT - 1))
                    mm.then_inc(sem("norm_sum"), 1)

            def head(h):
                W = lambda name, k: head_wait(pe, name, h, k)
                pe.wait_ge(sem("head"), h + 1)
                next_modulation(h, range(0, 3))
                for n, i in enumerate((1, 0)):
                    W("sqr", n + 1)
                    wide_mm(i, ones[:, :], pp[:, i, :, :].rearrange("p t c -> p (t c)"), "ssum")
                next_modulation(h, range(3, MOD_PER_HEAD))
                for d in (1, 0):
                    W("hsq", 2)
                    W("trig", 2)
                    wide_mm(d, ones[:, :], pp[:, d, :, :].rearrange("p t c -> p (t c)"), "grow")
                W("kn", 1)
                kk = lambda t: cv[:, 1, t * P:(t + 1) * P]
                tile_mm(2, kk, kk, "gram")
                W("silu", 3)
                for t in range(TT):
                    mm = pe.transpose(wide(3)[:, t * P:(t + 1) * P], cv[:, 2, t * P:(t + 1) * P], ident)
                mm.then_inc(sem("tok_t"), 1)
                for l in range(6):
                    for d in range(2):
                        W("ml", 2 * l + d + 1)
                        if l == 0:
                            W("er", 2)
                            W("dm", 10)
                            tile_mm(2 * d, lambda t: ml[:, d, t, :], lambda t: ident, "p")
                        else:
                            W("xup", 2 * l - 1 + d)
                            W("xtup", 2 * l - 1 + d)
                            tile_mm(2 * d, lambda t: ml[:, d, t, :], lambda t: xx[:, d, t, :], "p")
                    if l == 0:
                        for t in range(TT):
                            mm = pe.transpose(wide(1)[:, t * P:(t + 1) * P], kk(t), ident)
                        mm.then_inc(sem("tok_t"), 1)
                        W("qn", 1)
                        W("vtok", 1)
                        tile_mm(3, kk, lambda t: cv[:, 0, t * P:(t + 1) * P], "qk")
                        W("intra", 2)
                        W("ktok", 1)
                    if l == 0:
                        continue
                    for d in range(2):
                        W("pcopy", 2 * l - 1 + d)
                        if l < 5:
                            tile_mm(2 * d + 1, lambda t: xt[:, d, t, :], lambda t: pp[:, d, t, :], "xm")
                        tile_mm(2 * d, lambda t: pp[:, d, t, :], lambda t: xt[:, d, t, :], "xtm")
                for j in range(10):
                    for d in range(2):
                        kind, t, hh = order(d)[j]
                        R = slice(CH * hh, CH * hh + CH)
                        cols = slice(t * P + CH * hh, t * P + CH * hh + CH)
                        if j == 0:
                            W("xtup", 12)
                            W("xup", 10)
                            W("sz", 1)
                            W("s_init", 32)
                        elif j != 2:
                            W(f"sup{d}", j)
                        if j > 0:
                            W(f"vp{d}", j)
                        pe.matmul(psum[R, 4 * d, 0:P], cv[:, 1, cols], st[:, kind, d, :],
                                  start=True, stop=True).then_inc(sem(f"ks{d}"), 1)
                    for d in range(2):
                        kind, t, hh = order(d)[j]
                        cols = slice(t * P + CH * hh, t * P + CH * hh + CH)
                        W("qe", 2)
                        if j > 0:
                            W(f"ocp{d}", j)
                        pe.matmul(psum[:, 4 * d + 2, 0:CH], st[:, kind, d, :], qe[:, d, cols], start=True, stop=False)
                    for d in range(2):
                        kind, t, hh = order(d)[j]
                        R = slice(CH * hh, CH * hh + CH)
                        W(f"vp{d}", j + 1)
                        if j > 0:
                            W(f"vn{d}", j)
                        pe.matmul(psum[:, 4 * d + 1, 0:P], xt[R, d, t, :], vp[R, d, :],
                                  start=True, stop=True).then_inc(sem(f"vnm{d}"), 1)
                    for d in range(2):
                        kind, t, hh = order(d)[j]
                        R = slice(CH * hh, CH * hh + CH)
                        cols = slice(t * P + CH * hh, t * P + CH * hh + CH)
                        W(f"vn{d}", j + 1)
                        W(f"ke", 2)
                        if j > 0:
                            W(f"sup{d}", j)
                        pe.matmul(psum[:, 4 * d + 3, 0:P], ke[R, d, t, :], vn[R, d, :],
                                  start=True, stop=True).then_inc(sem(f"dsm{d}"), 1)
                        pe.matmul(psum[:, 4 * d + 2, 0:CH], vn[R, d, :], it[R, d, t, R],
                                  start=False, stop=True).then_inc(sem(f"om{d}"), 1)
                W("osq", 1)
                wide_mm(0, ones[:, :], pp[:, 0, :, :].rearrange("p t c -> p (t c)"), "omm")

            def expert(u0, hidden):
                with pe.Fori(0, 5) as i:
                    for s in range(2):
                        unit(i * 2 + u0 + s, s, KT, 2, a_hi, a_lo)
                unit(u0 + 10, 0, KT, 2, a_hi, a_lo)
                for n, m0, nm in DOWN:
                    if n == 0:
                        pe.wait_ge(sem("act_lo"), hidden + (FT + 1))
                    unit(u0 + 11 + n, (11 + n) % 2, FT, nm, act_hi, act_lo)

            def gather(x):
                pe.wait_ge(sem("picked"), x + 1)
                for b in range(4):
                    for k in (2 * b, 2 * b + 1):
                        for n, src in enumerate((ht_hi, ht_lo)):
                            for t in range(TT):
                                mm = pe.matmul(psum[:, b, (k % 2) * CAP:(k % 2 + 1) * CAP],
                                               src[:, t, k * P:(k + 1) * P], pick[:, t, :],
                                               start=(n == 0 and t == 0), stop=(n == 1 and t == TT - 1))
                    mm.then_inc(sem("gathered"), 1)

            def turn_back(x):
                for i, s0, ns in SLOTS:
                    for t in range(TT):
                        pe.transpose(wide(i)[0:ns, t * P:(t + 1) * P], pick[:, t, s0:s0 + ns].bitcast(F32), ident)
                for i, s0, ns in SLOTS:
                    for t in range(TT):
                        mm = pe.matmul(psum[0:ns, 2 * i + 1, 256:257], pick[:, t, s0:s0 + ns].bitcast(F32),
                                       g_now[:, t:t + 1], start=(t == 0), stop=(t == TT - 1))
                mm.then_inc(sem("turned"), 1)

            def scatter(x):
                pe.wait_ge(sem("y_split"), x * 2 + 2)
                for m in range(KT):
                    if m >= 2:
                        pe.wait_ge(sem("added"), x * KT + (m + 1))
                    for n, (i, s0, ns) in enumerate(SLOTS):
                        for v, src in enumerate((y_hi, y_lo)):
                            for c0, c1 in ((0, 512), (512, T)):
                                mm = pe.matmul(wide(2 + m % 2)[:, c0:c1], src[0:ns, i, m * P:(m + 1) * P],
                                               back[0:ns, i, c0:c1], start=(n == 0 and v == 0), stop=(n == 1 and v == 1))
                    mm.then_inc(sem("scattered"), 1)

            def routed(x):
                for j in range(M_UNITS):
                    q = j % 3
                    if j == 2:
                        scatter(x)
                    pe.wait_ge(sem(f"m_split{j % 2}"), x * (M_UNITS // 2) + (j // 2 + 2))
                    wh, wl = m_hi[q], m_lo[q]
                    if j < FT:
                        if j == 0:
                            pe.wait_ge(sem("he_lo"), x * 4 + 4)
                        if j >= 3:
                            pe.wait_ge(sem("m_prod"), x * FT + (j - 1))
                        for g in range(2):
                            for k in range(KT):
                                c = (2 * k + g) * P
                                for n, (w, v) in enumerate(((wh, he_hi), (wh, he_lo), (wl, he_hi))):
                                    mm = pe.matmul(psum[:, q, g * CAP:(g + 1) * CAP], w[:, c:c + P], v[:, k, :],
                                                   start=(k == 0 and n == 0), stop=(k == KT - 1 and n == 2))
                        mm.then_inc(sem("multiplied"), 1)
                        continue
                    k0, nk = DOWN_K[j - FT]
                    if j == FT:
                        pe.wait_ge(sem("m_prod"), x * FT + (FT + 1))
                        pe.wait_ge(sem("g_now"), x + 1)
                        turn_back(x)
                        pe.wait_ge(sem("hid_lo"), x * FT + FT)
                        pe.wait_ge(sem("added"), x * KT + (KT + 2))
                    if j == FT + 1:
                        pe.wait_ge(sem("turned_out"), x * 2 + 2)
                        gather(x + 1)
                    for k in range(nk):
                        for i, s0, ns in SLOTS:
                            for n, (v, w) in enumerate(((hid_hi, wh), (hid_hi, wl), (hid_lo, wh))):
                                for a in range(2):
                                    mm = pe.matmul(psum[0:ns, 4 + 2 * i + a, :], v[:, k0 + k, s0:s0 + ns],
                                                   w[:, k * D + 512 * a:k * D + 512 * a + 512],
                                                   start=(k0 + k == 0 and n == 0), stop=(k0 + k == FT - 1 and n == 2))
                    mm.then_inc(sem("multiplied"), 1)

            pe.wait_ge(sem("params"), 16 * 16)
            pe.wait_ge(sem("masks"), 1)
            pe.wait_ge(sem("ones"), 1)
            pe.transpose(psum[:, 6, 0:N_PAR1], par1[:, :], ident)
            pe.transpose(psum[:, 7, 0:N_PAR2], par2[0:N_PAR2, :], same[0:N_PAR2, 0, 0:N_PAR2])\
                .then_inc(sem("cols_t"), 1)
            for t in range(TT):
                if t >= 2:
                    pe.wait_ge(sem("x_evac"), t - 1)
                for k in range(KT):
                    mm = pe.transpose(psum[:, 2 + 2 * (t % 2) + k // 4, (k % 4) * P:(k % 4 + 1) * P],
                                      xtok[:, t, k * P:(k + 1) * P], ident)
                mm.then_inc(sem("x_t"), 1)
            modulation()
            pe.wait_ge(sem("mod_evac"), 1)
            norm(0)
            pe.wait_ge(sem("h_lo"), KT)
            pe.wait_ge(sem("h_hi"), 2 * KT)
            pe.wait_ge(sem("x_evac"), TT)
            square_units(8, U_DN_IN, a_hi, a_lo)
            pe.wait_ge(sem("wab_lo"), 1)
            pe.wait_ge(sem("evacuated"), N_DN_IN)
            for t in range(TT):
                for k in range(KT):
                    for n, (x_, w_) in enumerate(((a_hi, wab_hi), (a_hi, wab_lo), (a_lo, wab_hi))):
                        mm = pe.matmul(psum[:, 0, t * 32:(t + 1) * 32], x_[:, k, t * P:(t + 1) * P], w_[:, k, :],
                                       start=(k == 0 and n == 0), stop=(k == KT - 1 and n == 2))
            mm.then_inc(sem("ab_mm"), 1)
            pe.wait_ge(sem("g_ready"), 1)
            for d in range(2):
                pe.matmul(psum[:, 2, 40 * d:40 * d + 40], tri[:, d, :],
                          tab[:, 0, d, :, :].rearrange("p h t -> p (h t)"), start=True, stop=True)
            pe.matmul(psum[:, 3, 0:80], same[:, 6, :], tab[:, 0, :, :, :].rearrange("p d h t -> p (d h t)"),
                      start=True, stop=True).then_inc(sem("gc_mm"), 1)
            pe.wait_ge(sem("tab"), 3)
            with pe.Fori(0, H) as h:
                head(h)
            pe.wait_ge(sem("head"), H + 1)
            pe.wait_ge(sem("act_lo"), 1)
            square_units(2, U_DN_OUT, act_hi, act_lo)
            norm(1)
            pe.wait_ge(sem("h_lo"), 2 * KT)
            with pe.Fori(0, N_FFN) as e:
                expert(e * PER_EXPERT + U_FFN, e * FT)
            pe.wait_ge(sem("evacuated"), U_SC_IN)
            norm(2)
            pe.wait_ge(sem("h_lo"), 3 * KT)
            square_units(6, U_SC_IN, a_hi, a_lo)
            pe.wait_ge(sem("cy_split"), 2)
            square_units(2, U_SC_OUT, a_hi, a_lo)
            norm(3)
            pe.wait_ge(sem("h_lo"), 4 * KT)
            for n, src in enumerate((a_hi, a_lo)):
                for t in range(TT):
                    i = n * TT + t
                    if i >= 2:
                        pe.wait_ge(sem("ht"), i - 1)
                    for k in range(KT):
                        mm = pe.transpose(psum[:, 4 + 2 * (i % 2) + k // 4, (k % 4) * P:(k % 4 + 1) * P],
                                          src[:, k, t * P:(t + 1) * P].bitcast(F32), ident)
                    mm.then_inc(sem("ht_t"), 1)
            pe.wait_ge(sem("wrt_lo"), 1)
            for t in range(TT):
                for k in range(KT):
                    for n, (x_, w_) in enumerate(((a_hi, wrt_hi), (a_hi, wrt_lo), (a_lo, wrt_hi))):
                        mm = pe.matmul(psum[:, 2, t * E:(t + 1) * E], x_[:, k, t * P:(t + 1) * P], w_[:, k, :],
                                       start=(k == 0 and n == 0), stop=(k == KT - 1 and n == 2))
            mm.then_inc(sem("router_mm"), 1)
            pe.wait_ge(sem("sel"), 1)
            pe.matmul(psum[:, 0, 0:TT * E], earlier[:, :], sel[:, :, :].rearrange("p t e -> p (t e)"),
                      start=True, stop=True)
            pe.matmul(psum[:, 1, 0:TT * E], ones[:, :], sel[:, :, :].rearrange("p t e -> p (t e)"),
                      start=True, stop=True).then_inc(sem("counted"), 1)
            pe.wait_ge(sem("items"), 1)
            pe.wait_ge(sem("ht"), 2 * TT)
            n_items = pe.value_load(items[0:1, MAX_ITEMS + 1:MAX_ITEMS + 2], min_val=1, max_val=MAX_ITEMS)
            gather(0)
            with pe.Fori(0, n_items) as x:
                routed(x)
            scatter(n_items)
            norm(4)
            for t in range(TT):
                if t == 0:
                    pe.wait_ge(sem("y_scaled"), 2 * KT)
                if t >= 2:
                    pe.wait_ge(sem("y_evac"), t - 1)
                for k in range(KT):
                    mm = pe.transpose(psum[:, 2 + 2 * (t % 2) + k // 4, (k % 4) * P:(k % 4 + 1) * P],
                                      yT[:, k, t * P:(t + 1) * P], ident)
                mm.then_inc(sem("y_t"), 1)

        @block.scalar
        def _(act):
            def norm(q, ready, count):
                act.wait_ge(sem(ready), count)
                for k in range(KT):
                    if k >= 2:
                        act.wait_ge(sem("norm_sum"), KT * q + k - 1)
                    act.activation(sq[:, k % 2, :], xT[:, k, :], ACT.Square).then_inc(sem("squared"), 1)
                act.wait_ge(sem("norm_sum"), KT * (q + 1))
                act.activation(two(ms[:, :]), halves(0), ACT.Sqrt, scale=1.0 / D, bias=eps[:, :])\
                    .then_inc(sem("rms"), 1)

            def norm_hi(q, n):
                for k in range(KT):
                    for i, (c0, c1, w) in enumerate(SPANS):
                        act.wait_ge(sem("h_scaled"), 2 * (KT * q + k) + i + 1)
                        act.activation(a_hi[:, k, c0:c1], hp[:, k % 2, c0:c1], ACT.Identity,
                                       bias=mod[:, 24 * n + k, w:w + 1]).then_inc(sem("h_hi"), 1)

            def evac_stage(u, i, s):
                act.wait_ge(sem("multiplied"), u + 1)
                if i is not None:
                    act.wait_ge(sem(f"stored{s}"), i * 16)
                act.activation(stage[:, s, :, :].rearrange("p m (a c) -> p (m a) c", a=2),
                               psum[:, 4 * s:4 * s + 4, 0:HALF], ACT.Copy).then_inc(sem("evacuated"), 1)
                act.wait_ge(sem("evacuated"), u + 1)
                act.dma_start(scratch.rearrange("(u m) p t -> u p m t", m=2)[bass.ds(u, 1)]
                              .rearrange("o p m t -> p (o m) t"), stage[:, s, :, :]).then_inc(sem(f"stored{s}"), 16)

            def fetch(h):
                act.dma_start(praw[:, :, :], scratch.rearrange("(g h) p t -> h p g t", g=4)[bass.ds(h, 1)]
                              .rearrange("o p g t -> p (o g) t")).then_inc(sem("raw"), 32)

            def head(h, more):
                W = lambda name, k: head_wait(act, name, h, k)
                act.wait_ge(sem("head"), h + 1)
                for d, src in enumerate((state_fwd, state_bwd)):
                    act.dma_start(st[:, 1, d, :], src[0, 0, bass.ds(h, 1)].rearrange("o k v -> (o k) v"))\
                        .then_inc(sem("s_init"), 16)
                for n, i in enumerate((1, 0)):
                    W("conv", 5 * (n + 1))
                    act.activation(cv[:, i, :], cv[:, i, :], ACT.Silu).then_inc(sem("silu"), 1)
                    W("silu", n + 1)
                    act.activation(pp[:, i, :, :].rearrange("p t c -> p (t c)"), cv[:, i, :], ACT.Square)\
                        .then_inc(sem("sqr"), 1)
                W("conv", 15)
                act.activation(cv[:, 2, :], cv[:, 2, :], ACT.Silu).then_inc(sem("silu"), 1)
                W("raw", 32)
                act.activation(zs[:, :], praw[:, 3, :], ACT.Silu).then_inc(sem("silu"), 1)
                for n, dst in enumerate((er[:, 1, :], qe[:, 0, :])):
                    W("ssum", n + 1)
                    act.activation(dst, wide(1 - n), ACT.Sqrt, bias=eps[:, :]).then_inc(sem("hsq"), 1)
                if more:
                    W("silu", 4)
                    fetch(h + 1)
                for d in (1, 0):
                    W("grow", 2 - d)
                    W("dm", 10 - 5 * d)
                    W("kn", 1)
                    act.activation(ee[:, d, :, :], ee[:, d, :, :], ACT.Exp).then_inc(sem("ex"), 1)
                for d in (1, 0):
                    act.activation(er[:, d, :], wide(d), ACT.Exp).then_inc(sem("er"), 1)
                W("tok_t", 1)
                act.activation(vtok[:, :, :], tiles(wide(3)), ACT.Copy).then_inc(sem("vtok"), 1)
                W("tok_t", 2)
                act.activation(ktok[:, :, :], tiles(wide(1)), ACT.Copy).then_inc(sem("ktok"), 1)
                for l in range(1, 6):
                    for d in range(2):
                        W("p", 2 * l + d + 1)
                        act.activation(pp[:, d, :, :], tiles(wide(2 * d)), ACT.Copy).then_inc(sem("pcopy"), 1)
                for j in range(10):
                    for d in range(2):
                        kind, t, hh = order(d)[j]
                        R = slice(CH * hh, CH * hh + CH)
                        W(f"vnm{d}", j + 1)
                        if j > 0:
                            W(f"om{d}", j)
                        act.activation(vn[R, d, :], psum[R, 4 * d + 1, 0:P], ACT.Copy,
                                       scale=hcol[R, 1, d, t:t + 1]).then_inc(sem(f"vn{d}"), 1)
                    for d in range(2):
                        kind, t, hh = order(d)[j]
                        cols = slice(t * P + CH * hh, t * P + CH * hh + CH)
                        W(f"om{d}", j + 1)
                        act.activation(ot[:, d, cols], psum[:, 4 * d + 2, 0:CH], ACT.Copy).then_inc(sem(f"ocp{d}"), 1)
                for d, dst in enumerate((new_fwd, new_bwd)):
                    W(f"sup{d}", 2)
                    act.dma_start(dst[0, 0, bass.ds(h, 1)].rearrange("o k v -> (o k) v"), st[:, 0, d, :])\
                        .then_inc(sem("st_out"), 16)
                W("st_out", 32)
                W("osum", 1)
                act.activation(pp[:, 0, :, :].rearrange("p t c -> p (t c)"), ot[:, 0, :], ACT.Square)\
                    .then_inc(sem("osq"), 1)
                W("omm", 1)
                act.activation(er[:, 0, :], wide(0), ACT.Sqrt, scale=1.0 / P, bias=eps[:, :]).then_inc(sem("hsq"), 1)

            def gate_unit(u, s, j):
                act.wait_ge(sem("multiplied"), u + 1)
                act.wait_ge(sem("evacuated"), u)
                act.activation(two(sg[:, :]), halves(4 * s), ACT.Silu).then_inc(sem("silu_g"), 1)
                act.wait_ge(sem("evacuated"), u + 1)
                act.activation(act_hi[:, bass.ds(j, 1), :].rearrange("p o c -> p (o c)"), prod[:, :],
                               ACT.Copy).then_inc(sem("act_hi"), 1)

            def expert(u0):
                with act.Fori(0, 5) as i:
                    for s in range(2):
                        gate_unit(i * 2 + u0 + s, s, i * 2 + s)
                gate_unit(u0 + 10, 0, FT - 1)

            act.wait_ge(sem("masks"), 1)
            act.wait_ge(sem("ones"), 1)
            act.wait_ge(sem("cols"), 1)
            for w in range(2):
                act.activation(cond[:, :, w], col1[:, C_COND + 8 * w:C_COND + 8 * w + 8], ACT.Silu)\
                    .then_inc(sem("cond"), 1)
            act.wait_ge(sem("params"), 16 * 16)
            act.activation(wab_hi[:, :, :], wab[:, :, :], ACT.Copy).then_inc(sem("wab_hi"), 1)
            act.activation(wrt_hi[:, :, :], wrt[:, :, :], ACT.Copy).then_inc(sem("wrt_hi"), 1)
            norm(0, "x_evac", TT)
            act.wait_ge(sem("alpha"), 2)
            norm_hi(0, 0)
            for s in range(2):
                evac_stage(s, None, s)
            with act.Fori(1, N_DN_IN // 2) as i:
                for s in range(2):
                    evac_stage(i * 2 + s, i, s)
            act.wait_ge(sem("negabs"), 1)
            act.activation(small[:, 1, :], small[:, 1, :], ACT.Exp).then_inc(sem("e_negabs"), 1)
            act.wait_ge(sem("e_negabs"), 1)
            act.activation(small[:, 1, :], small[:, 1, :], ACT.Ln, bias=ones[:, 0:1]).then_inc(sem("ln1p"), 1)
            act.activation(alog[:, :], alog[:, :], ACT.Exp).then_inc(sem("ea"), 1)
            act.wait_ge(sem("ab_mm"), 1)
            act.wait_ge(sem("ab_read"), 1)
            act.activation(small[:, 3, :].rearrange("p (t c) -> p t c", t=TT),
                           psum[:, 0, 0:160].rearrange("p (t c) -> p t c", t=TT)[:, :, 16:32], ACT.Exp,
                           scale=-1.0).then_inc(sem("e_b"), 1)
            act.wait_ge(sem("gc"), 1)
            act.activation(small[:, 4, :], small[:, 4, :], ACT.Exp).then_inc(sem("e_gc"), 1)
            act.wait_ge(sem("gdiff"), 1)
            act.activation(tab[:, 4, :, :, :].rearrange("p d h t -> p (d h t)"), small[:, 5, :], ACT.Exp)\
                .then_inc(sem("tab"), 1)
            act.wait_ge(sem("stored0"), 16 * 8)
            act.wait_ge(sem("stored1"), 16 * 8)
            act.wait_ge(sem("tab"), 3)
            fetch(0)
            with act.Fori(0, H - 1) as h:
                head(h, True)
            head(H - 1, False)
            act.wait_ge(sem("head"), H + 1)
            act.activation(act_hi[:, 0:H, :], oall[:, :, :], ACT.Copy).then_inc(sem("o_hi"), 1)
            norm(1, "evacuated", U_FFN)
            norm_hi(1, 1)
            with act.Fori(0, N_FFN) as e:
                expert(e * PER_EXPERT + U_FFN)
            norm(2, "evacuated", U_SC_IN)
            act.wait_ge(sem("alpha"), 4)
            norm_hi(2, 0)
            with act.Fori(0, 2) as i:
                for s in range(2):
                    u = i * 2 + (U_SC_IN + s)
                    act.wait_ge(sem("multiplied"), u + 1)
                    act.activation(cu[:, bass.ds(i * 4 + 2 * s, 2), :].rearrange("p m (a c) -> p (m a) c", a=2),
                                   psum[:, 4 * s:4 * s + 4, 0:HALF], ACT.Copy).then_inc(sem("evacuated"), 1)
            act.wait_ge(sem("evacuated"), U_SC_IN + N_SC_IN)
            act.activation(a_hi[:, :, :], cy[:, :, :], ACT.Copy).then_inc(sem("cy_hi"), 1)
            norm(3, "evacuated", U_MOE)
            norm_hi(3, 1)
            for i in range(2 * TT):
                act.wait_ge(sem("ht_t"), i + 1)
                act.activation((ht_hi if i < TT else ht_lo)[:, i % TT, :], psum[:, 4 + 2 * (i % 2):6 + 2 * (i % 2), :]
                               .rearrange("p b c -> p (b c)"), ACT.Copy).then_inc(sem("ht"), 1)
            act.wait_ge(sem("rt_shift"), 1)
            act.activation(sm[:, 1, :, :], sm[:, 1, :, :], ACT.Exp).then_inc(sem("rt_exp"), 1)

            def gathered(x):
                for b in range(4):
                    act.wait_ge(sem("gathered"), x * 4 + (b + 1))
                    act.activation(he_hi[:, 2 * b:2 * b + 2, :].rearrange("p k c -> p (k c)"), psum[:, b, 0:2 * CAP],
                                   ACT.Copy).then_inc(sem("he_hi"), 1)

            def m_high(x, j):
                n, q = m_cols(j), j % 3
                act.wait_ge(sem(f"m_loaded{j % 2}"), x * (16 * M_UNITS) + 32 * (j // 2 + 1))
                act.wait_ge(sem("multiplied"), x * M_UNITS + (U_MOE + j - 2))
                act.activation(m_hi[q][:, 0:n], m_raw[j % 2][:, 0:n], ACT.Copy).then_inc(sem("m_high"), 1)

            def routed(x):
                for j in range(M_UNITS):
                    if j + 2 < M_UNITS:
                        m_high(x, j + 2)
                    else:
                        m_high(x + 1, j + 2 - M_UNITS)
                    if j < FT:
                        act.wait_ge(sem("multiplied"), x * M_UNITS + (U_MOE + j + 1))
                        act.wait_ge(sem("m_prod"), x * FT + (j + 1))
                        act.activation(m_sg[:, :], psum[:, j % 3, 0:CAP], ACT.Silu).then_inc(sem("m_silu"), 1)
                        act.wait_ge(sem("m_prod"), x * FT + (j + 2))
                        act.activation(hid_hi[:, j, :], m_prod[:, :], ACT.Copy).then_inc(sem("hid_hi"), 1)
                    if j == FT:
                        act.wait_ge(sem("turned"), x + 1)
                        for i, s0, ns in SLOTS:
                            act.activation(g_slot[0:ns, i:i + 1], psum[0:ns, 2 * i + 1, 256:257], ACT.Copy)\
                                .then_inc(sem("g_slot"), 1)
                            act.activation(back[0:ns, i, :], wide(i)[0:ns, :], ACT.Copy).then_inc(sem("turned_out"), 1)
                    if j == FT + 1:
                        gathered(x + 1)
                act.wait_ge(sem("multiplied"), x * M_UNITS + (U_MOE + M_UNITS))
                act.wait_ge(sem("g_slot"), x * 2 + 2)
                for i, s0, ns in SLOTS:
                    act.activation(y_hi[0:ns, i, :], psum[0:ns, 4 + 2 * i:6 + 2 * i, :].rearrange("p b c -> p (b c)"),
                                   ACT.Copy, scale=g_slot[0:ns, i:i + 1]).then_inc(sem("y_hi"), 1)

            act.wait_ge(sem("items"), 1)
            n_items = act.value_load(items[0:1, MAX_ITEMS + 1:MAX_ITEMS + 2], min_val=1, max_val=MAX_ITEMS)
            gathered(0)
            m_high(0, 0)
            m_high(0, 1)
            with act.Fori(0, n_items) as x:
                routed(x)
            norm(4, "moe_done", 1)

        @block.vector
        def _(dve):
            def norm(q, w_of, out=None):
                dve.wait_ge(sem("rms"), q + 1)
                dve.reciprocal(rstd[:, :], ms[:, :]).then_inc(sem("rstd"), 1)
                dve.wait_ge(sem("rstd"), q + 1)
                n = q % 2

                def scaled(k):
                    if out is None and k >= 2:
                        dve.wait_ge(sem("h_lo"), KT * q + k - 1)
                    for c0, c1, w in SPANS:
                        dst = hp[:, k % 2, c0:c1] if out is None else out[:, k, c0:c1]
                        dve.scalar_tensor_tensor(out=dst, in0=xT[:, k, c0:c1], scalar=w_of(k, w), in1=rstd[:, c0:c1],
                                                 op0=ALU.mult, op1=ALU.mult)\
                            .then_inc(sem("h_scaled" if out is None else "y_scaled"), 1)

                def rest(k):
                    for i, (c0, c1, w) in enumerate(SPANS):
                        dve.wait_ge(sem("h_hi"), 2 * (KT * q + k) + i + 1)
                        ins = dve.scalar_tensor_tensor(out=a_lo[:, k, c0:c1], in0=hp[:, k % 2, c0:c1],
                                                       scalar=mod[:, 24 * n + k, w:w + 1],
                                                       in1=a_hi[:, k, c0:c1].bitcast(F32),
                                                       op0=ALU.add, op1=ALU.subtract)
                    ins.then_inc(sem("h_lo"), 1)

                scaled(0)
                if out is None:
                    for k in range(KT):
                        if k + 1 < KT:
                            scaled(k + 1)
                        rest(k)
                else:
                    for k in range(1, KT):
                        scaled(k)

            def modulation(layer):
                dve.wait_ge(sem("mod_used"), N_MOD if layer == 0 else N_MOD + H * MOD_PER_HEAD)
                bank, c0 = (0, 0) if layer == 0 else (7, MOD_COL)
                if layer == 1:
                    dve.wait_ge(sem("evacuated"), U_SC_IN)
                b = col2[:, C_MODB + 48 * layer:C_MODB + 48 * layer + 48].unsqueeze(2).broadcast_to([P, 48, 2])
                dve.tensor_tensor(mod[:, :, :], psum[:, bank, c0:c0 + 96].rearrange("p (m w) -> p m w", w=2), b, ALU.add)\
                    .then_inc(sem("mod_evac"), 1)
                dve.wait_ge(sem("mod_evac"), layer + 1)
                for n in range(2):
                    nw = col1[:, C_NORM + 16 * layer + 8 * n:C_NORM + 16 * layer + 8 * n + 8]\
                        .unsqueeze(2).broadcast_to([P, KT, 2])
                    dve.scalar_tensor_tensor(out=alpha[:, n, :, :], in0=mod[:, 24 * n + 8:24 * n + 16, :], scalar=1.0,
                                             in1=nw, op0=ALU.add, op1=ALU.mult).then_inc(sem("alpha"), 1)
                dve.wait_ge(sem("alpha"), 2 * layer + 2)

            def a_of(n):
                return lambda k, w: alpha[:, n, k, w:w + 1]

            PIECES = [(0, 0, TC, 0), (0, TC, HALF - TC, 1), (1, 0, HALF, 1)]

            def residual(u, s, m_of, nm, gmod, last=None):
                dve.wait_ge(sem("multiplied"), u + 1)
                for m in range(nm):
                    for b, c0, n, w in PIECES:
                        xs = xT[:, bass.ds(m_of + m, 1), b * HALF + c0:b * HALF + c0 + n]\
                            .rearrange("p o c -> p (o c)")
                        ins = dve.scalar_tensor_tensor(out=xs, in0=psum[:, 4 * s + 2 * m + b, c0:c0 + n],
                                                       scalar=mod[:, bass.ds(m_of + (gmod + m), 1), w], in1=xs,
                                                       op0=ALU.mult, op1=ALU.add)
                ins.then_inc(sem("evacuated"), 1)

            def out_units(u0, gmod):
                with dve.Fori(0, 2) as i:
                    for s in range(2):
                        residual(i * 2 + (u0 + s), s, i * 4 + 2 * s, 2, gmod)

            def gate_unit(u, s, j, n0):
                dve.wait_ge(sem("silu_g"), n0 + 1)
                dve.wait_ge(sem("act_lo"), n0 + 1)
                dve.tensor_tensor(two(prod[:, :]), two(sg[:, :]), halves(4 * s + 2), ALU.mult)\
                    .then_inc(sem("evacuated"), 1)
                dve.wait_ge(sem("act_hi"), n0 + 1)
                dve.tensor_tensor(act_lo[:, bass.ds(j, 1), :].rearrange("p o c -> p (o c)"), prod[:, :],
                                  act_hi[:, bass.ds(j, 1), :].rearrange("p o c -> p (o c)").bitcast(F32),
                                  ALU.subtract).then_inc(sem("act_lo"), 1)

            def expert(u0, n0):
                with dve.Fori(0, 5) as i:
                    for s in range(2):
                        gate_unit(i * 2 + u0 + s, s, i * 2 + s, i * 2 + n0 + s)
                gate_unit(u0 + 10, 0, FT - 1, n0 + 10)
                for n, m0, nm in DOWN:
                    u, s = u0 + 11 + n, (11 + n) % 2
                    dve.wait_ge(sem("evacuated"), u)
                    dve.wait_ge(sem("multiplied"), u + 1)
                    for m in range(nm):
                        for b, c0, w_, w in PIECES:
                            xs = xT[:, m0 + m, b * HALF + c0:b * HALF + c0 + w_]
                            ins = dve.scalar_tensor_tensor(out=xs, in0=psum[:, 4 * s + 2 * m + b, c0:c0 + w_],
                                                           scalar=mod[:, 40 + m0 + m, w:w + 1], in1=xs,
                                                           op0=ALU.mult, op1=ALU.add)
                    ins.then_inc(sem("evacuated"), 1)

            def conv(dst, src, w, tag, n0):
                def lat(ap):
                    return ap[:, TC:T].rearrange("p (r c) -> p r c", c=GRID)
                dve.tensor_scalar(dst, src, w(1), None, ALU.mult).then_inc(sem(tag), 1)
                dve.wait_ge(sem(tag), n0 + 1)
                taps = [(dst[:, 1:TC], src[:, 0:TC - 1], w(0)),
                        (lat(dst)[:, :, 1:GRID], lat(src)[:, :, 0:GRID - 1], w(0)),
                        (dst[:, 0:TC - 1], src[:, 1:TC], w(2)),
                        (lat(dst)[:, :, 0:GRID - 1], lat(src)[:, :, 1:GRID], w(2))]
                for i, (o_, i_, wt) in enumerate(taps):
                    if i == 2:
                        dve.wait_ge(sem(tag), n0 + 3)
                    dve.scalar_tensor_tensor(out=o_, in0=i_, scalar=wt, in1=o_, op0=ALU.mult, op1=ALU.add)\
                        .then_inc(sem(tag), 1)

            def head(h):
                W = lambda name, k: head_wait(dve, name, h, k)
                dve.tensor_copy(hcol[:, :, :, :].rearrange("p q d t -> p (q d) t"),
                                tab[:, :, :, bass.ds(h, 1), :].rearrange("p q d o t -> p (q d) (o t)"))\
                    .then_inc(sem("hcol"), 1)
                dve.tensor_copy(hconv[:, :, :],
                                col1[:, C_CONV:C_CONV + 72].rearrange("p (j i h) -> p j i h", j=3, i=3)
                                [:, :, :, bass.ds(h, 1)].rearrange("p j i o -> p j (i o)")).then_inc(sem("hcol"), 1)
                W("hcol", 2)
                W("raw", 32)
                for n, i in enumerate((1, 0, 2)):
                    conv(cv[:, i, :], praw[:, i, :], lambda j: hconv[:, j, i:i + 1], "conv",
                         h * PER_HEAD["conv"] + 5 * n)
                dve.memset(st[:, 0, :, :], 0.0).then_inc(sem("sz"), 1)
                for d in range(2):
                    W("ssum", 2)
                    dve.tensor_tensor(pp[:, d, :, :], tri[:, d, :].unsqueeze(1).broadcast_to([P, TT, P]),
                                      hcol[:, 0, d, :].unsqueeze(2).broadcast_to([P, TT, P]), ALU.mult)\
                        .then_inc(sem("trig"), 1)

                def unit_norm(n, i, root, nm, sc):
                    W("hsq", n + 1)
                    dve.reciprocal(root, root).then_inc(sem("rs"), 1)
                    W("rs", n + 1)
                    W("sqr", n + 1)
                    dve.scalar_tensor_tensor(out=cv[:, i, :], in0=cv[:, i, :], scalar=sc, in1=root,
                                             op0=ALU.mult, op1=ALU.mult).then_inc(sem(nm), 1)

                unit_norm(0, 1, er[:, 1, :], "kn", 1.0)
                for d in (1, 0):
                    W("grow", 2 - d)
                    for t in range(TT):
                        dve.tensor_scalar(ee[:, d, t, :], wide(d)[:, t * P:(t + 1) * P], hcol[:, 2, d, t:t + 1], 0.0,
                                          ALU.subtract, ALU.min).then_inc(sem("dm"), 1)
                for d in (1, 0):
                    W("ex", 2 - d)
                    dve.tensor_tensor(ee[:, d, :, :], ee[:, d, :, :],
                                      tri[:, d, :].unsqueeze(1).broadcast_to([P, TT, P]), ALU.mult)\
                        .then_inc(sem("em"), 1)
                W("gram", 1)
                for d in range(2):
                    W("em", 2)
                    for t in range(TT):
                        dve.scalar_tensor_tensor(out=lt[:, d, t, :], in0=wide(2)[:, t * P:(t + 1) * P],
                                                 scalar=hcol[:, 1, d, t:t + 1], in1=ee[:, d, t, :],
                                                 op0=ALU.mult, op1=ALU.mult).then_inc(sem("lt"), 1)
                idb = ident.unsqueeze(1).broadcast_to([P, TT, P])
                for d in range(2):
                    W("lt", 5 * d + 5)
                    dve.tensor_tensor(ml[:, d, :, :], lt[:, d, :, :],
                                      level[:, 0, :].unsqueeze(1).broadcast_to([P, TT, P]), ALU.mult)\
                        .then_inc(sem("ml"), 1)
                for d in range(2):
                    W("ml", d + 1)
                    dve.tensor_tensor(xt[:, d, :, :], idb, ml[:, d, :, :], ALU.subtract).then_inc(sem("xtup"), 1)
                unit_norm(1, 0, qe[:, 0, :], "qn", QK_SCALE)
                for d in range(2):
                    W("p", d + 1)
                    dve.tensor_tensor(xx[:, d, :, :], idb, tiles(wide(2 * d)), ALU.subtract).then_inc(sem("xup"), 1)
                W("qk", 1)
                for d in range(2):
                    dve.tensor_tensor(it[:, d, :, :], tiles(wide(3)), ee[:, d, :, :], ALU.mult)\
                        .then_inc(sem("intra"), 1)
                for l in range(1, 6):
                    for d in range(2):
                        W("xtm", 2 * (l - 1) + d + 1)
                        if l < 5:
                            W("xm", 2 * (l - 1) + d + 1)
                            W("xup", 2 * l - 1 + d)
                            dve.tensor_tensor(xx[:, d, :, :], xx[:, d, :, :], tiles(wide(2 * d + 1)), ALU.subtract)\
                                .then_inc(sem("xup"), 1)
                        W("xtup", 2 * l - 1 + d)
                        dve.tensor_tensor(xt[:, d, :, :], xt[:, d, :, :], tiles(wide(2 * d)), ALU.subtract)\
                            .then_inc(sem("xtup"), 1)
                for j in range(10):
                    for d in range(2):
                        kind, t, hh = order(d)[j]
                        R = slice(CH * hh, CH * hh + CH)
                        W(f"ks{d}", j + 1)
                        W("vtok", 1)
                        if j > 0:
                            W(f"vnm{d}", j)
                        dve.scalar_tensor_tensor(out=vp[R, d, :], in0=psum[R, 4 * d, 0:P],
                                                 scalar=hcol[R, 3, d, t:t + 1], in1=vtok[R, t, :],
                                                 op0=ALU.mult, op1=ALU.add).then_inc(sem(f"vp{d}"), 1)
                    for d in range(2):
                        kind, t, hh = order(d)[j]
                        last = t * P + CH * hh + (CH - 1 if d == 0 else 0)
                        W(f"dsm{d}", j + 1)
                        if j > 0:
                            W(f"sup{d}", j)
                        dve.scalar_tensor_tensor(out=st[:, kind, d, :], in0=st[:, kind, d, :],
                                                 scalar=er[:, d, last:last + 1], in1=psum[:, 4 * d + 3, 0:P],
                                                 op0=ALU.mult, op1=ALU.add).then_inc(sem(f"sup{d}"), 1)
                W("ocp0", 10)
                W("ocp1", 10)
                dve.tensor_tensor(ot[:, 0, :], ot[:, 0, :], ot[:, 1, :], ALU.add).then_inc(sem("osum"), 1)
                W("hsq", 3)
                dve.reciprocal(er[:, 0, :], er[:, 0, :]).then_inc(sem("ors"), 1)
                W("ors", 1)
                dve.scalar_tensor_tensor(out=er[:, 1, :], in0=ot[:, 0, :],
                                         scalar=col2[:, C_DNNORM:C_DNNORM + 1], in1=er[:, 0, :],
                                         op0=ALU.mult, op1=ALU.mult).then_inc(sem("onrm"), 1)
                W("onrm", 1)
                dve.tensor_tensor(oall[:, bass.ds(h, 1), :].rearrange("p o c -> p (o c)"), er[:, 1, :], zs[:, :],
                                  ALU.mult).then_inc(sem("head"), 1)
                dve.wait_ge(sem("head"), h + 2)

            dve.wait_ge(sem("cols_t"), 1)
            dve.tensor_copy(col1[:, :], psum[:, 6, 0:N_PAR1]).then_inc(sem("col1"), 1)
            dve.tensor_copy(col2[:, :], psum[:, 7, 0:N_PAR2]).then_inc(sem("cols"), 1)
            dve.wait_ge(sem("cols"), 1)
            for t in range(TT):
                dve.wait_ge(sem("x_t"), t + 1)
                b = 2 + 2 * (t % 2)
                dve.tensor_copy(xT[:, :, t * P:(t + 1) * P],
                                psum[:, b:b + 2, :].rearrange("p b (k c) -> p (b k) c", c=P)).then_inc(sem("x_evac"), 1)
            dve.wait_ge(sem("x_evac"), TT)
            for hi, lo, w, tag in ((wab_hi, wab_lo, wab, "wab"), (wrt_hi, wrt_lo, wrt, "wrt")):
                dve.wait_ge(sem(tag + "_hi"), 1)
                dve.tensor_tensor(lo[:, :, :], w[:, :, :], hi[:, :, :].bitcast(F32), ALU.subtract)\
                    .then_inc(sem(tag + "_lo"), 1)
            modulation(0)
            norm(0, a_of(0))
            dve.wait_ge(sem("ab_mm"), 1)
            ab = psum[:, 0, 0:160].rearrange("p (t c) -> p t c", t=TT)
            tv = lambda i: small[:, i, :].rearrange("p (t c) -> p t c", t=TT)
            dve.tensor_tensor(tv(0), ab[:, :, 0:16], dtb[:, :].unsqueeze(1).broadcast_to([P, TT, 2 * H]), ALU.add)\
                .then_inc(sem("ab_read"), 1)
            dve.wait_ge(sem("ab_read"), 1)
            dve.tensor_scalar(small[:, 1, :], small[:, 0, :], -1.0, None, ALU.mult).then_inc(sem("gate_step"), 1)
            dve.tensor_scalar(small[:, 2, :], small[:, 0, :], 0.0, None, ALU.max).then_inc(sem("gate_step"), 1)
            dve.wait_ge(sem("gate_step"), 1)
            dve.tensor_tensor(small[:, 1, :], small[:, 1, :], small[:, 0, :], ALU.min).then_inc(sem("negabs"), 1)
            dve.wait_ge(sem("ln1p"), 1)
            dve.wait_ge(sem("gate_step"), 2)
            dve.tensor_tensor(small[:, 2, :], small[:, 2, :], small[:, 1, :], ALU.add).then_inc(sem("gate_step"), 1)
            dve.wait_ge(sem("gate_step"), 3)
            dve.wait_ge(sem("ea"), 1)
            dve.scalar_tensor_tensor(out=tv(0), in0=tv(2), scalar=-1.0,
                                     in1=alog[:, :].unsqueeze(1).broadcast_to([P, TT, 2 * H]),
                                     op0=ALU.mult, op1=ALU.mult).then_inc(sem("gate_step"), 1)
            dve.wait_ge(sem("gate_step"), 4)
            dve.tensor_copy(tab[:, 0, :, :, :].rearrange("p d h t -> p (d h) t"),
                            tv(0).rearrange("p t c -> p c t")).then_inc(sem("g_ready"), 1)
            dve.wait_ge(sem("e_b"), 1)
            dve.tensor_scalar(small[:, 3, :], small[:, 3, :], 1.0, None, ALU.add).then_inc(sem("gate_step"), 1)
            dve.wait_ge(sem("gate_step"), 5)
            dve.reciprocal(small[:, 3, :], small[:, 3, :]).then_inc(sem("gate_step"), 1)
            dve.wait_ge(sem("gate_step"), 6)
            dve.tensor_copy(tab[:, 1, :, :, :].rearrange("p d h t -> p (d h) t"),
                            tv(3).rearrange("p t c -> p c t")).then_inc(sem("tab"), 1)
            dve.wait_ge(sem("gc_mm"), 1)
            gcol = tab[:, 2, :, :, :].rearrange("p d h t -> p (d h t)")
            dve.tensor_copy(gcol, psum[:, 2, 0:80]).then_inc(sem("gate_step"), 1)
            dve.wait_ge(sem("gate_step"), 7)
            dve.tensor_copy(small[:, 4, :], gcol).then_inc(sem("gc"), 1)
            dve.tensor_tensor(small[:, 5, :], psum[:, 3, 0:80], gcol, ALU.subtract).then_inc(sem("gdiff"), 1)
            dve.wait_ge(sem("e_gc"), 1)
            dve.tensor_scalar(tab[:, 3, :, :, :].rearrange("p d h t -> p (d h t)"), small[:, 4, :], -1.0, None,
                              ALU.mult).then_inc(sem("tab"), 1)
            dve.wait_ge(sem("tab"), 3)
            dve.memset(st[:, 0, :, :], 0.0).then_inc(sem("head"), 1)
            dve.wait_ge(sem("head"), 1)
            with dve.Fori(0, H) as h:
                head(h)
            dve.wait_ge(sem("o_hi"), 1)
            dve.tensor_tensor(act_lo[:, 0:H, :], oall[:, :, :], act_hi[:, 0:H, :].bitcast(F32), ALU.subtract)\
                .then_inc(sem("act_lo"), 1)
            out_units(U_DN_OUT, 16)
            norm(1, a_of(1))
            with dve.Fori(0, N_FFN) as e:
                expert(e * PER_EXPERT + U_FFN, e * FT)
            modulation(1)
            norm(2, a_of(0))
            with dve.Fori(0, 2) as i:
                for s in range(2):
                    u = i * 2 + (U_SC_IN + 4 + s)
                    dve.wait_ge(sem("multiplied"), u + 1)
                    dve.wait_ge(sem("evacuated"), U_SC_IN + 4)
                    v = cu[:, bass.ds(i * 4 + 2 * s, 2), :].rearrange("p m (a c) -> p (m a) c", a=2)
                    dve.tensor_tensor(v, v, psum[:, 4 * s:4 * s + 4, 0:HALF], ALU.mult).then_inc(sem("evacuated"), 1)
            dve.wait_ge(sem("evacuated"), U_SC_IN + 8)
            for k in range(KT):
                conv(cy[:, k, :], cu[:, k, :],
                     lambda j: col2[:, C_SCCONV + 8 * j + k:C_SCCONV + 8 * j + k + 1], "sconv", 5 * k)
            dve.wait_ge(sem("sconv"), 5 * KT)
            with dve.Fori(0, 2) as i:
                for s in range(2):
                    u = i * 2 + (U_SC_IN + 8 + s)
                    dve.wait_ge(sem("multiplied"), u + 1)
                    v = cy[:, bass.ds(i * 4 + 2 * s, 2), :].rearrange("p m (a c) -> p (m a) c", a=2)
                    dve.tensor_tensor(v, v, psum[:, 4 * s:4 * s + 4, 0:HALF], ALU.mult).then_inc(sem("evacuated"), 1)
            dve.wait_ge(sem("cy_hi"), 1)
            dve.tensor_tensor(a_lo[:, :, :], cy[:, :, :], a_hi[:, :, :].bitcast(F32), ALU.subtract)\
                .then_inc(sem("cy_split"), 2)
            out_units(U_SC_OUT, 16)
            norm(3, a_of(1))
            dve.wait_ge(sem("router_mm"), 1)
            rt = [0]

            def step(ins):
                rt[0] += 1
                ins.then_inc(sem("rt"), 1)
                dve.wait_ge(sem("rt"), rt[0])

            lg = sm[:, 0, :, :]
            red = lambda i: sm[:, 5, :, i:i + 1]
            wideE = lambda ap: ap.broadcast_to([P, TT, E])
            step(dve.tensor_tensor(lg, psum[:, 2, 0:TT * E].rearrange("p (t e) -> p t e", e=E),
                                   rtb[:, :].unsqueeze(1).broadcast_to([P, TT, E]), ALU.add))
            step(dve.tensor_reduce(red(0).rearrange("p t o -> p (t o)"), lg, AX.X, ALU.max))
            dve.tensor_tensor(sm[:, 1, :, :], lg, wideE(red(0)), ALU.subtract).then_inc(sem("rt_shift"), 1)
            dve.wait_ge(sem("rt_exp"), 1)
            step(dve.tensor_reduce(red(1).rearrange("p t o -> p (t o)"), sm[:, 1, :, :], AX.X, ALU.add))
            step(dve.reciprocal(red(2), red(1)))
            step(dve.tensor_tensor(sm[:, 2, :, :], sm[:, 1, :, :], wideE(red(2)), ALU.mult))
            pe_ = sm[:, 2, :, :].unsqueeze(3).broadcast_to([P, TT, E, E])
            pf_ = sm[:, 2, :, :].unsqueeze(2).broadcast_to([P, TT, E, E])
            step(dve.memset(before[:, :, :], 0.0))
            for e in range(1, E):
                step(dve.memset(before[:, e, 0:e], 1.0))
            for t in range(TT):
                step(dve.tensor_tensor(cmp_gt[:, t], pf_[:, t], pe_[:, t], ALU.is_gt))
                step(dve.tensor_tensor(cmp_eq[:, t], pf_[:, t], pe_[:, t], ALU.is_equal))
            step(dve.tensor_tensor(cmp_eq[:, :, :, :].rearrange("p t e f -> p t (e f)"),
                                   cmp_eq[:, :, :, :].rearrange("p t e f -> p t (e f)"),
                                   before[:, :, :].rearrange("p e f -> p (e f)").unsqueeze(1)
                                   .broadcast_to([P, TT, E * E]), ALU.mult))
            step(dve.tensor_tensor(cmp_gt[:, :, :, :], cmp_gt[:, :, :, :], cmp_eq[:, :, :, :], ALU.add))
            step(dve.tensor_reduce(sm[:, 3, :, :].rearrange("p t e -> p (t e)"),
                                   cmp_gt[:, :, :, :].rearrange("p t e f -> p (t e) f"), AX.X, ALU.add))
            step(dve.scalar_tensor_tensor(out=sm[:, 4, :, :], in0=sm[:, 3, :, :], scalar=2.0, in1=sm[:, 2, :, :],
                                          op0=ALU.is_lt, op1=ALU.mult))
            step(dve.tensor_reduce(red(3).rearrange("p t o -> p (t o)"), sm[:, 4, :, :], AX.X, ALU.add))
            step(dve.reciprocal(red(4), red(3)))
            step(dve.tensor_tensor(gates[:, :, :], sm[:, 4, :, :], wideE(red(4)), ALU.mult))
            step(dve.tensor_scalar(sel[:, :, :], sm[:, 3, :, :], 2.0, None, ALU.is_lt))
            dve.memset(cum[:, 0, :], 0.0).then_inc(sem("sel"), 1)
            dve.wait_ge(sem("sel"), 1)
            dve.wait_ge(sem("counted"), 1)
            for t in range(TT):
                step(dve.tensor_tensor(cum[:, t + 1, :], cum[:, t, :], psum[:, 1, t * E:(t + 1) * E], ALU.add))
            pos = slot_of[:, :, 0:E]
            step(dve.tensor_tensor(pos, psum[:, 0, 0:TT * E].rearrange("p (t e) -> p t e", e=E), cum[:, 0:TT, :],
                                   ALU.add))
            step(dve.scalar_tensor_tensor(out=pos, in0=pos, scalar=FAR, in1=sel[:, :, :], op0=ALU.add, op1=ALU.mult))
            step(dve.tensor_scalar(pos, pos, -FAR, None, ALU.add))
            dve.wait_ge(sem("slots"), 1)
            step(dve.tensor_scalar(n_of[:, 0, :], cum[:, TT, :], 0.0, None, ALU.is_gt))
            for i in range(1, MAX_PASS):
                step(dve.tensor_scalar(n_of[:, 1, :], cum[:, TT, :], float(i * CAP), None, ALU.is_gt))
                step(dve.tensor_tensor(n_of[:, 0, :], n_of[:, 0, :], n_of[:, 1, :], ALU.add))
            step(dve.memset(first[:, 0:1], 0.0))
            for e in range(E):
                step(dve.tensor_tensor(first[:, e + 1:e + 2], first[:, e:e + 1], n_of[:, 0, e:e + 1], ALU.add))
            NI = MAX_ITEMS + 1
            per_e = lambda ap: ap.unsqueeze(1).broadcast_to([P, NI, E])
            step(dve.tensor_tensor(nth[:, :, :], slots[:, 0:NI].unsqueeze(2).broadcast_to([P, NI, E]),
                                   per_e(first[:, 0:E]), ALU.subtract))
            step(dve.tensor_scalar(mine[:, :, :], nth[:, :, :], 0.0, None, ALU.is_ge))
            step(dve.tensor_tensor(picked[:, :, :], per_e(n_of[:, 0, :]), nth[:, :, :], ALU.is_gt))
            step(dve.tensor_tensor(mine[:, :, :], mine[:, :, :], picked[:, :, :], ALU.mult))
            step(dve.tensor_tensor(picked[:, :, :], mine[:, :, :], per_e(slots[:, 0:E]), ALU.mult))
            step(dve.tensor_reduce(item_e[:, :], picked[:, :, :], AX.X, ALU.add))
            step(dve.tensor_scalar(nth[:, :, :], nth[:, :, :], -float(CAP), None, ALU.mult))
            for t in range(TT):
                step(dve.tensor_tensor(picked[:, :, :], mine[:, :, :], per_e(gates[:, t, :]), ALU.mult))
                step(dve.tensor_reduce(item_gate[:, t, :], picked[:, :, :], AX.X, ALU.add))
                step(dve.tensor_tensor(picked[:, :, :], nth[:, :, :], per_e(slot_of[:, t, :]), ALU.add))
                step(dve.tensor_tensor(picked[:, :, :], picked[:, :, :], mine[:, :, :], ALU.mult))
                step(dve.tensor_reduce(item_slot[:, t, :], picked[:, :, :], AX.X, ALU.add))
            step(dve.tensor_copy(items[:, 0:NI], item_e[:, :]))
            dve.tensor_copy(items[:, NI:NI + 1], first[:, E:E + 1]).then_inc(sem("items"), 1)
            dve.wait_ge(sem("items"), 1)
            dve.wait_ge(sem("ht"), 2 * TT)
            dve.memset(m_lo[1][:, 0:1].bitcast(F32), 0.0).then_inc(sem("m_split1"), 1)
            n_items = dve.value_load(items[0:1, MAX_ITEMS + 1:MAX_ITEMS + 2], min_val=1, max_val=MAX_ITEMS)
            dve.memset(m_prod[:, :], 0.0).then_inc(sem("m_prod"), 1)
            for _ in range(2):
                dve.memset(small[:, 0, 0:1], 0.0).then_inc(sem("added"), 1)
                dve.wait_ge(sem("added"), _ + 1)

            def pick_tokens(x):
                for t in range(TT):
                    ins = dve.tensor_scalar(pick[:, t, :], slots[:, :], item_slot[:, t, bass.ds(x, 1)], None,
                                            ALU.is_equal)
                ins.then_inc(sem("picked"), 1)

            def gathered_low(x):
                for b in range(4):
                    dve.wait_ge(sem("he_hi"), x * 4 + (b + 1))
                    dve.tensor_tensor(he_lo[:, 2 * b:2 * b + 2, :].rearrange("p k c -> p (k c)"),
                                      psum[:, b, 0:2 * CAP],
                                      he_hi[:, 2 * b:2 * b + 2, :].rearrange("p k c -> p (k c)").bitcast(F32),
                                      ALU.subtract).then_inc(sem("he_lo"), 1)

            def add_scattered(x):
                for m in range(KT):
                    dve.wait_ge(sem("scattered"), x * KT + (m + 1))
                    for c0, c1, w in SPANS:
                        ins = dve.scalar_tensor_tensor(out=xT[:, m, c0:c1], in0=wide(2 + m % 2)[:, c0:c1],
                                                       scalar=mod[:, 40 + m, w:w + 1], in1=xT[:, m, c0:c1],
                                                       op0=ALU.mult, op1=ALU.add)
                    ins.then_inc(sem("added"), 1)

            def routed(x):
                dve.tensor_copy(g_now[:, :], item_gate[:, :, bass.ds(x, 1)].rearrange("p t o -> p (t o)"))\
                    .then_inc(sem("g_now"), 1)
                for j in range(M_UNITS):
                    if j == 2:
                        add_scattered(x)
                    if j < FT:
                        dve.wait_ge(sem("m_silu"), x * FT + (j + 1))
                        if j > 0:
                            dve.wait_ge(sem("hid_lo"), x * FT + j)
                        dve.tensor_tensor(m_prod[:, :], m_sg[:, :], psum[:, j % 3, CAP:2 * CAP], ALU.mult)\
                            .then_inc(sem("m_prod"), 1)
                        dve.wait_ge(sem("hid_hi"), x * FT + (j + 1))
                        dve.tensor_tensor(hid_lo[:, j, :], m_prod[:, :], hid_hi[:, j, :].bitcast(F32), ALU.subtract)\
                            .then_inc(sem("hid_lo"), 1)
                    if j == M_UNITS - 1:
                        m_low(dve, x + 1, 1)
                    elif j % 2:
                        m_low(dve, x, j + 2)
                    if j == FT:
                        dve.wait_ge(sem("turned"), x + 1)
                        pick_tokens(x + 1)
                    if j == FT + 1:
                        gathered_low(x + 1)
                for i, s0, ns in SLOTS:
                    dve.wait_ge(sem("y_hi"), x * 2 + (i + 1))
                    dve.scalar_tensor_tensor(out=y_lo[0:ns, i, :],
                                             in0=psum[0:ns, 4 + 2 * i:6 + 2 * i, :].rearrange("p b c -> p (b c)"),
                                             scalar=g_slot[0:ns, i:i + 1], in1=y_hi[0:ns, i, :].bitcast(F32),
                                             op0=ALU.mult, op1=ALU.subtract).then_inc(sem("y_split"), 1)
            pick_tokens(0)
            gathered_low(0)
            m_low(dve, 0, 1)
            with dve.Fori(0, n_items) as x:
                routed(x)
            add_scattered(n_items)
            dve.memset(small[:, 0, 0:1], 0.0).then_inc(sem("moe_done"), 1)
            norm(4, lambda k, w: col1[:, C_FINAL + k:C_FINAL + k + 1], out=yT)
            for t in range(TT):
                dve.wait_ge(sem("y_t"), t + 1)
                b = 2 + 2 * (t % 2)
                dve.tensor_copy(ytok[:, t, :].rearrange("p (k c) -> p k c", c=P),
                                psum[:, b:b + 2, :].rearrange("p b (k c) -> p (b k) c", c=P)).then_inc(sem("y_evac"), 1)


_INS = ['x_prompt', 'x_sample', 'state_fwd', 'state_bwd', 'c', 'c_ctx', 'norm_w', 'mod_w', 'mod_b', 'dn_w_in',
        'dn_conv', 'dn_a_log', 'dn_dt_bias', 'dn_norm', 'dn_w_out', 'sc_w_in', 'sc_conv', 'sc_w_out', 'ffn_w13',
        'ffn_w2', 'moe_router', 'moe_router_b', 'moe_w13', 'moe_w2', 'final_norm']
_OUTS = [((1, 128, 1024), 'float32'), ((1, 512, 1024), 'float32'),
         ((1, 1, 8, 128, 128), 'float32'), ((1, 1, 8, 128, 128), 'float32')]


def kernel(**inputs):
    import numpy as _np
    import concourse.bacc as _bacc
    from concourse import mybir as _mybir
    from concourse.bass_utils import run_bass_kernel_spmd as _run

    nc = _bacc.Bacc("TRN2", target_bir_lowering=False, num_devices=1)
    arrays, args = {}, []
    for name in _INS:
        a = _np.ascontiguousarray(inputs[name])
        arrays[f"in_{name}_dram"] = a
        args.append(nc.dram_tensor(f"in_{name}_dram", a.shape, _mybir.dt.from_np(a.dtype), kind="ExternalInput").ap())
    for i, (shape, dtype) in enumerate(_OUTS):
        dt = _mybir.dt.from_np(_np.dtype(dtype))
        args.append(nc.dram_tensor(f"out_{i}_dram", shape, dt, kind="ExternalOutput").ap())
    build(nc, *args)
    r = _run(nc, [arrays], core_ids=[0])
    return tuple(r.results[0][f"out_{i}_dram"] for i in range(len(_OUTS)))
```
